# Optimizing a Trainium2 kernel written in Bass

```python
import math, functools
import jax, jax.numpy as jnp
from jax import lax
import numpy as np

D_MODEL = 1024
BATCH = 1
SEQ = 1024
DEPTH = 1
DEC_BATCH = 8
DEC_SEQ = 8
PAST_LEN = 1024
PAGE_SIZE = 128

D_RNN = D_MODEL
N_RNN_BLOCKS = 8
RNN_BLOCK = D_RNN // N_RNN_BLOCKS
CONV_W = 4
RG_C = 8.0
N_HEADS = 8
HEAD_DIM = 64
KV_DIM = 2 * HEAD_DIM
D_ATTN = N_HEADS * KV_DIM
D_FF = 3 * D_MODEL
FFN_CONV_W = 3
N_BUCKETS = 32
MAX_DISTANCE = 128
Q_BLOCK = 128
EPS = 1e-6
D_IN = D_RNN + 3 * D_ATTN + 2 * D_MODEL

kernel_name = 'hawk_diffattn_gated_merge_convffn_step'

def rms_norm(x, g):
    xf = x.astype(jnp.float32)
    y = xf * lax.rsqrt(jnp.mean(xf * xf, axis=-1, keepdims=True) + EPS)
    return (y * g.astype(jnp.float32)).astype(x.dtype)

def causal_dwconv(x, buf, w, b):
    width = w.shape[0]
    t = x.shape[1]
    xe = jnp.concatenate([buf.astype(x.dtype), x], axis=1)
    y = b
    for kk in range(width):
        y = y + w[kk] * xe[:, kk:kk + t]
    return y.astype(x.dtype), xe[:, -(width - 1):]

def _lin_combine(c1, c2):
    a1, b1 = c1
    a2, b2 = c2
    return a1 * a2, a2 * b1 + b2

def rg_lru(x, pos, h0, w_a, b_a, w_x, b_x, a_param):
    bsz, t, c = x.shape
    xb = x.reshape(bsz, t, N_RNN_BLOCKS, RNN_BLOCK)
    gate_a = jnp.einsum('btnc,ncd->btnd', xb, w_a).reshape(bsz, t, c) + b_a
    gate_x = jnp.einsum('btnc,ncd->btnd', xb, w_x).reshape(bsz, t, c) + b_x
    r = jax.nn.sigmoid(gate_a.astype(jnp.float32))
    i = jax.nn.sigmoid(gate_x.astype(jnp.float32))
    log_a = -RG_C * r * jax.nn.softplus(-a_param.astype(jnp.float32))
    reset = (pos == 0)[None, :, None]
    a = jnp.where(reset, 0.0, jnp.exp(log_a))
    mult = jnp.where(reset, 1.0, jnp.sqrt(-jnp.expm1(2.0 * log_a)))
    bterm = mult * i * x.astype(jnp.float32)
    a_cum, h = lax.associative_scan(_lin_combine, (a, bterm), axis=1)
    h = h + a_cum * h0.astype(jnp.float32)[:, None]
    return h.astype(x.dtype), h[:, -1].astype(x.dtype)

def rel_bucket(dist):
    n = jnp.maximum(dist, 0)
    max_exact = N_BUCKETS // 2
    nf = jnp.maximum(n, 1).astype(jnp.float32)
    large = max_exact + (jnp.log(nf / max_exact) / math.log(MAX_DISTANCE / max_exact)
                         * (N_BUCKETS - max_exact)).astype(jnp.int32)
    large = jnp.minimum(large, N_BUCKETS - 1)
    return jnp.where(n < max_exact, n, large)

def diff_logits(q, q_pos, k, k_pos, rel_bias):
    s = jnp.einsum('bqhmd,bkhmd->bhmqk', q, k).astype(jnp.float32) * (HEAD_DIM ** -0.5)
    dist = q_pos[:, None] - k_pos[None, :]
    bias = jnp.transpose(rel_bias[rel_bucket(dist)], (2, 0, 1)).astype(jnp.float32)
    s = s + bias[None, :, None]
    return jnp.where((dist >= 0)[None, None, None], s, -1e30)

def diff_weights(logits, lam):
    p = jax.nn.softmax(logits, axis=-1)
    return p[:, :, 0] - lam * p[:, :, 1]

def prompt_attn(q, k, v, lam, rel_bias):
    bsz, t = q.shape[:2]
    nb = t // Q_BLOCK
    k_pos = jnp.arange(t, dtype=jnp.int32)
    qb = q.reshape(bsz, nb, Q_BLOCK, N_HEADS, 2, HEAD_DIM).transpose(1, 0, 2, 3, 4, 5)
    qpos = k_pos.reshape(nb, Q_BLOCK)

    def one_block(args):
        qi, pi = args
        w = diff_weights(diff_logits(qi, pi, k, k_pos, rel_bias), lam)
        return jnp.einsum('bhqk,bkhe->bqhe', w.astype(v.dtype), v)

    o = lax.map(one_block, (qb, qpos))
    return o.transpose(1, 0, 2, 3, 4).reshape(bsz, t, N_HEADS, KV_DIM)

def sample_attn(q, k, v, lam, k_past, v_past, rel_bias):
    t = q.shape[1]
    past = k_past.shape[1]
    q_pos = past + jnp.arange(t, dtype=jnp.int32)
    s_past = diff_logits(q, q_pos, k_past, jnp.arange(past, dtype=jnp.int32), rel_bias)
    s_new = diff_logits(q, q_pos, k, q_pos, rel_bias)
    w = diff_weights(jnp.concatenate([s_past, s_new], axis=-1), lam).astype(v.dtype)
    return (jnp.einsum('bhqk,bkhe->bqhe', w[..., :past], v_past)
            + jnp.einsum('bhqk,bkhe->bqhe', w[..., past:], v))

def layer(x, pos, rnn_h0, rnn_buf, ffn_buf, attend, lp, lambda_init):
    bsz, t, _ = x.shape
    h = rms_norm(x, lp['norm_attn'])
    proj = jnp.einsum('btd,de->bte', h, lp['w_in'])
    o0 = D_RNN
    o1 = o0 + D_ATTN
    o2 = o1 + D_ATTN
    o3 = o2 + D_ATTN
    o4 = o3 + D_MODEL
    x_r = proj[..., :o0]
    q = proj[..., o0:o1].reshape(bsz, t, N_HEADS, 2, HEAD_DIM)
    k = proj[..., o1:o2].reshape(bsz, t, N_HEADS, 2, HEAD_DIM)
    v = proj[..., o2:o3].reshape(bsz, t, N_HEADS, KV_DIM)
    g_a = jax.nn.sigmoid(proj[..., o3:o4])
    g_b = jax.nn.sigmoid(proj[..., o4:])
    x_c, new_rnn_buf = causal_dwconv(x_r, rnn_buf, lp['conv_w'], lp['conv_b'])
    y_a, h_last = rg_lru(x_c, pos, rnn_h0, lp['rg_w_a'], lp['rg_b_a'], lp['rg_w_x'],
                         lp['rg_b_x'], lp['rg_a_param'])
    f32 = jnp.float32
    lam = (jnp.exp(jnp.sum(lp['lq1'].astype(f32) * lp['lk1'].astype(f32)))
           - jnp.exp(jnp.sum(lp['lq2'].astype(f32) * lp['lk2'].astype(f32))) + lambda_init)
    o = attend(q, k, v, lam)
    y_b = (rms_norm(o, lp['subln_g']) * (1.0 - lambda_init)).reshape(bsz, t, D_ATTN)
    x = x + jnp.einsum('btd,de->bte', g_a * y_a + g_b * y_b, lp['w_out'])
    h2 = rms_norm(x, lp['norm_ffn'])
    up = jnp.einsum('btd,df->btf', h2, lp['w_up'])
    up_c, new_ffn_buf = causal_dwconv(up, ffn_buf, lp['ffn_conv_w'], lp['ffn_conv_b'])
    act = jax.nn.gelu(up_c[..., :D_FF]) * up_c[..., D_FF:]
    x = x + jnp.einsum('btf,fd->btd', act, lp['w_down'])
    return x, k.reshape(bsz, t, N_HEADS, KV_DIM), v, h_last, new_rnn_buf, new_ffn_buf

def setup_inputs(seed: int = 0) -> dict:
    key = jax.random.key(seed)
    ks = jax.random.split(key, 32)
    f32 = jnp.float32
    n_pages = PAST_LEN // PAGE_SIZE
    n_used = DEC_BATCH * n_pages
    n_pool = (n_used * 5) // 4
    nrm = lambda k, shape, s: (jax.random.normal(k, shape, f32) * s)
    a0 = jax.random.uniform(ks[10], (DEPTH, D_RNN), f32, 0.9, 0.999)
    return {
        'x_prompt': nrm(ks[0], (BATCH, SEQ, D_MODEL), 1.0),
        'x_sample': nrm(ks[1], (DEC_BATCH, DEC_SEQ, D_MODEL), 1.0),
        'cache_k': nrm(ks[2], (DEPTH, n_pool, PAGE_SIZE, N_HEADS, KV_DIM), 1.0),
        'cache_v': nrm(ks[3], (DEPTH, n_pool, PAGE_SIZE, N_HEADS, KV_DIM), 1.0),
        'page_table': jax.random.permutation(ks[4], n_pool)[:n_used].reshape(DEC_BATCH, n_pages).astype(jnp.int32),
        'state_rglru_h': nrm(ks[5], (DEPTH, DEC_BATCH, D_RNN), 0.5),
        'state_rglru_conv': nrm(ks[6], (DEPTH, DEC_BATCH, CONV_W - 1, D_RNN), 1.0),
        'state_ffn_conv': nrm(ks[7], (DEPTH, DEC_BATCH, FFN_CONV_W - 1, 2 * D_FF), 1.0),
        'w_in': nrm(ks[8], (DEPTH, D_MODEL, D_IN), D_MODEL ** -0.5),
        'conv_w': nrm(ks[9], (DEPTH, CONV_W, D_RNN), CONV_W ** -0.5),
        'conv_b': nrm(ks[11], (DEPTH, D_RNN), 0.01),
        'rg_w_a': nrm(ks[12], (DEPTH, N_RNN_BLOCKS, RNN_BLOCK, RNN_BLOCK), RNN_BLOCK ** -0.5),
        'rg_b_a': nrm(ks[13], (DEPTH, D_RNN), 0.01),
        'rg_w_x': nrm(ks[14], (DEPTH, N_RNN_BLOCKS, RNN_BLOCK, RNN_BLOCK), RNN_BLOCK ** -0.5),
        'rg_b_x': nrm(ks[15], (DEPTH, D_RNN), 0.01),
        'rg_a_param': jnp.log(a0) - jnp.log1p(-a0),
        'lambda_q1': nrm(ks[16], (DEPTH, HEAD_DIM), 0.1),
        'lambda_k1': nrm(ks[17], (DEPTH, HEAD_DIM), 0.1),
        'lambda_q2': nrm(ks[18], (DEPTH, HEAD_DIM), 0.1),
        'lambda_k2': nrm(ks[19], (DEPTH, HEAD_DIM), 0.1),
        'subln_g': 1.0 + nrm(ks[20], (DEPTH, KV_DIM), 0.02),
        'rel_bias': nrm(ks[21], (N_BUCKETS, N_HEADS), 0.5),
        'w_out': nrm(ks[22], (DEPTH, D_MODEL, D_MODEL), D_MODEL ** -0.5),
        'norm_attn': 1.0 + nrm(ks[23], (DEPTH, D_MODEL), 0.02),
        'norm_ffn': 1.0 + nrm(ks[24], (DEPTH, D_MODEL), 0.02),
        'w_up': nrm(ks[25], (DEPTH, D_MODEL, 2 * D_FF), D_MODEL ** -0.5),
        'ffn_conv_w': nrm(ks[26], (DEPTH, FFN_CONV_W, 2 * D_FF), FFN_CONV_W ** -0.5),
        'ffn_conv_b': nrm(ks[27], (DEPTH, 2 * D_FF), 0.01),
        'w_down': nrm(ks[28], (DEPTH, D_FF, D_MODEL), D_FF ** -0.5),
        'norm_final': 1.0 + nrm(ks[29], (D_MODEL,), 0.02),
    }

def reference(x_prompt, x_sample, cache_k, cache_v, page_table, state_rglru_h, state_rglru_conv,
              state_ffn_conv, w_in, conv_w, conv_b, rg_w_a, rg_b_a, rg_w_x, rg_b_x, rg_a_param,
              lambda_q1, lambda_k1, lambda_q2, lambda_k2, subln_g, rel_bias, w_out, norm_attn,
              norm_ffn, w_up, ffn_conv_w, ffn_conv_b, w_down, norm_final):
    bsz, t = x_prompt.shape[:2]
    dbsz = x_sample.shape[0]
    tsz = x_sample.shape[1]
    past = page_table.shape[1] * cache_k.shape[2]
    pos_p = jnp.arange(t, dtype=jnp.int32)
    pos_s = past + jnp.arange(tsz, dtype=jnp.int32)
    yp, ys = x_prompt, x_sample
    kp_l, vp_l, ks_l, vs_l, hp_l, hs_l, rp_l, rs_l, fp_l, fs_l = ([] for _ in range(10))
    for l in range(DEPTH):
        lp = {'w_in': w_in[l], 'conv_w': conv_w[l], 'conv_b': conv_b[l], 'rg_w_a': rg_w_a[l],
              'rg_b_a': rg_b_a[l], 'rg_w_x': rg_w_x[l], 'rg_b_x': rg_b_x[l],
              'rg_a_param': rg_a_param[l], 'lq1': lambda_q1[l], 'lk1': lambda_k1[l],
              'lq2': lambda_q2[l], 'lk2': lambda_k2[l], 'subln_g': subln_g[l], 'w_out': w_out[l],
              'norm_attn': norm_attn[l], 'norm_ffn': norm_ffn[l], 'w_up': w_up[l],
              'ffn_conv_w': ffn_conv_w[l], 'ffn_conv_b': ffn_conv_b[l], 'w_down': w_down[l]}
        lambda_init = 0.8 - 0.6 * math.exp(-0.3 * l)
        yp, kp, vp, hp, rp, fp = layer(
            yp, pos_p, jnp.zeros((bsz, D_RNN), x_prompt.dtype),
            jnp.zeros((bsz, CONV_W - 1, D_RNN), x_prompt.dtype),
            jnp.zeros((bsz, FFN_CONV_W - 1, 2 * D_FF), x_prompt.dtype),
            functools.partial(prompt_attn, rel_bias=rel_bias), lp, lambda_init)
        k_past = cache_k[l][page_table].reshape(dbsz, past, N_HEADS, 2, HEAD_DIM)
        v_past = cache_v[l][page_table].reshape(dbsz, past, N_HEADS, KV_DIM)
        ys, ks_, vs_, hs, rs, fs = layer(
            ys, pos_s, state_rglru_h[l], state_rglru_conv[l], state_ffn_conv[l],
            functools.partial(sample_attn, k_past=k_past, v_past=v_past, rel_bias=rel_bias),
            lp, lambda_init)
        kp_l.append(kp); vp_l.append(vp); ks_l.append(ks_); vs_l.append(vs_)
        hp_l.append(hp); hs_l.append(hs); rp_l.append(rp); rs_l.append(rs)
        fp_l.append(fp); fs_l.append(fs)
    y_prompt = rms_norm(yp, norm_final)
    y_sample = rms_norm(ys, norm_final)
    return (y_prompt, y_sample, jnp.stack(kp_l), jnp.stack(vp_l), jnp.stack(ks_l), jnp.stack(vs_l),
            jnp.stack(hp_l), jnp.stack(hs_l), jnp.stack(rp_l), jnp.stack(rs_l),
            jnp.stack(fp_l), jnp.stack(fs_l))


_drawn_inputs = setup_inputs


def setup_inputs(seed=0):
    import zlib

    import numpy as np

    out = dict(_drawn_inputs(seed))
    spreads = {}
    factors = {'rg_b_a': 27.77,
     'rg_b_x': 23.731,
     'subln_g': 6.893,
     'norm_attn': 2.901,
     'norm_ffn': 2.877,
     'ffn_conv_b': 7.857,
     'norm_final': 8.556,
     'conv_b': 4.906}
    for name, (base, spread) in spreads.items():
        noise = np.random.default_rng([zlib.crc32(name.encode()), seed]).standard_normal(out[name].shape)
        drawn = base * np.exp(spread * noise) if base else spread * noise
        out[name] = __import__('jax').numpy.asarray(drawn.astype(out[name].dtype))
    for name, factor in factors.items():
        out[name] = (out[name] * factor).astype(out[name].dtype)
    return out
```

```python
import math
from contextlib import ExitStack, contextmanager

import numpy as np
import concourse.bass as bass
from concourse import mybir

F32 = mybir.dt.float32
F32R = mybir.dt.float32r
I32 = mybir.dt.int32
ALU = mybir.AluOpType
ACT = mybir.ActivationFunctionType

D = 1024
SEQ = 1024
DEC_B, DEC_T = 8, 8
NS = DEC_B * DEC_T
NTOK = SEQ + NS
PAST, PAGE = 1024, 128
NPAGES = PAST // PAGE
H, HD = 8, 64
KV = 2 * HD
CONV_W = 4
DFF = 3 * D
FCONV_W = 3
N_BUCKETS, MAX_DIST = 32, 128
EPS = 1e-6
RG_C = 8.0
LAMBDA_INIT = 0.8 - 0.6 * math.exp(-0.3 * 0)
KT = D // 128
NEG = -1e30

CHUNKS = [(0, 384), (384, 384), (768, 320)]
PROMPT_OF = [384, 384, 256]

U0 = PAST + DEC_T - 1
UW = 432
NU = 3 * UW
BW = SEQ + 128
NKEYS = PAST + DEC_T

ROW = {}
_at = 0
for _name, _n in (("conv_w", 4), ("conv_b", 1), ("rg_b_a", 1), ("rg_b_x", 1), ("rg_a_param", 1),
                  ("h0", DEC_B), ("conv_state", DEC_B * (CONV_W - 1))):
    ROW[_name] = (_at, _n)
    _at += _n
NROW = _at
FROW = FCONV_W + 1 + DEC_B * (FCONV_W - 1)

K_, Q_, V_, GA, XR, GB = range(6)
COL0 = [2 * D, D, 3 * D, 4 * D, 0, 5 * D]


def bucket_onehot():
    d = U0 - np.arange(NU)
    n = np.maximum(d, 0)
    exact = N_BUCKETS // 2
    nf = np.maximum(n, 1).astype(np.float32)
    large = exact + (np.log(nf / np.float32(exact)) / np.float32(math.log(MAX_DIST / exact))
                     * np.float32(N_BUCKETS - exact)).astype(np.int32)
    bucket = np.where(n < exact, n, np.minimum(large, N_BUCKETS - 1))
    bucket = np.where(d < 0, N_BUCKETS, bucket)
    return (np.arange(N_BUCKETS + 1)[:, None] == bucket[None, :]).astype(np.float32)


def flat(ap):
    names = " ".join(f"d{i}" for i in range(len(ap.shape) - 1))
    return ap.rearrange(f"{names} n -> ({names}) n")


def broadcast_row(ap, parts):
    n = 1
    for s in ap.shape:
        n *= s
    return bass.AP(tensor=ap.tensor, offset=ap.offset, ap=[[0, parts], [1, n]])


def norm_tiles(nc, sb, sem, name, load, gain, dst_hi, dst_lo, ident, ps, NT=9):
    xt = sb(name + "_xt", [128, 2, D], F32)
    xn = sb(name + "_xn", [128, 2, D], F32)
    junk = sb(name + "_junk", [128, D], F32)
    g = sb(name + "_g", [128, D], F32)
    st = sb(name + "_st", [128, 2, 3], F32)
    eps = sb(name + "_eps", [128, 1], F32)
    x_in = [sem(name + f"_x_in{u}") for u in range(2)]
    g_in = sem(name + "_g_in")
    eps_set = sem(name + "_eps_set")
    ssq_done = sem(name + "_ssq_done")
    std_done = sem(name + "_std_done")
    inv_done = sem(name + "_inv_done")
    xn_done = sem(name + "_xn_done")
    t_done = sem(name + "_t_done")
    hi_done = sem(name + "_hi_done")
    lo_done = sem(name + "_lo_done")

    def rows(t_is_sample):
        return NS if t_is_sample else 128

    def pairs(eng, body):
        with eng.Fori(0, 4) as i:
            body([2 * i, 2 * i + 1], False)
        body([8], True)

    with nc.Block() as block:
        @block.sync
        def _(sp):
            sp.dma_start(g[:, :], broadcast_row(gain, 128)).then_inc(g_in, 16)

            def body(ts, sample):
                for u, t in enumerate(ts):
                    sp.wait_ge(xn_done, t + 1)
                    load(sp, t, xt[0:rows(sample), u, :]).then_inc(x_in[u], 16)
            pairs(sp, body)

        @block.scalar
        def _(act):
            act.wait_ge(eps_set, 1)

            def body(ts, sample):
                n = rows(sample)
                for u, t in enumerate(ts):
                    act.wait_ge(x_in[u], 8 * (t - u) + 16)
                    act.activation(junk[0:n, :], xt[0:n, u, :], ACT.Square,
                                   accum_out=st[0:n, u, 0:1]).then_inc(ssq_done, 1)
                    act.wait_ge(ssq_done, t + 1)
                    act.activation(st[0:n, u, 1:2], st[0:n, u, 0:1], ACT.Sqrt, bias=eps[0:n, :],
                                   scale=1.0 / D).then_inc(std_done, 1)
                for u, t in enumerate(ts):
                    for q in range(2):
                        act.wait_ge(t_done, 2 * t + q + 1 + 4)
                        act.activation(
                            dst_hi[:, 4 * q:4 * q + 4, bass.ds(128 * t, n)],
                            ps[:, 2 * u + q, :].rearrange("p (k n) -> p k n", k=4)[:, :, 0:n],
                            ACT.Copy).then_inc(hi_done, 1)
            pairs(act, body)

        @block.vector
        def _(dve):
            dve.memset(eps[:, :], EPS).then_inc(eps_set, 1)
            dve.sem_inc(xn_done, 2)
            dve.sem_inc(lo_done, 4)
            dve.wait_ge(g_in, 16)

            def body(ts, sample):
                n = rows(sample)
                for u, t in enumerate(ts):
                    dve.wait_ge(std_done, t + 1)
                    dve.reciprocal(st[0:n, u, 2:3], st[0:n, u, 1:2]).then_inc(inv_done, 1)
                    dve.wait_ge(inv_done, t + 1)
                    dve.wait_ge(t_done, 2 * t + 2)
                    dve.scalar_tensor_tensor(out=xn[0:n, u, :], in0=xt[0:n, u, :], scalar=st[0:n, u, 2:3],
                                             in1=g[0:n, :], op0=ALU.mult, op1=ALU.mult).then_inc(xn_done, 1)
                for u, t in enumerate(ts):
                    for q in range(2):
                        dve.wait_ge(hi_done, 2 * t + q + 1)
                        cols = bass.ds(128 * t, n)
                        dve.tensor_tensor(
                            dst_lo[:, 4 * q:4 * q + 4, cols],
                            ps[:, 2 * u + q, :].rearrange("p (k n) -> p k n", k=4)[:, :, 0:n],
                            dst_hi[:, 4 * q:4 * q + 4, cols].bitcast(F32), ALU.subtract).then_inc(lo_done, 1)
            pairs(dve, body)

        @block.tensor
        def _(pe):
            pe.sem_inc(t_done, 4)

            def body(ts, sample):
                n = rows(sample)
                for u, t in enumerate(ts):
                    pe.wait_ge(xn_done, t + 1 + 2)
                    for q in range(2):
                        pe.wait_ge(lo_done, 2 * t + q + 1)
                        for k in range(4):
                            last = pe.transpose(ps[:, 2 * u + q, 128 * k:128 * k + n],
                                                xn[0:n, u, 512 * q + 128 * k:512 * q + 128 * (k + 1)],
                                                ident[0:n, 0:n])
                        last.then_inc(t_done, 1)
            pairs(pe, body)


def setup(nc, sb, sem, ins, c):
    prow = sb("prow", [NROW, D], F32)
    frow = sb("frow", [FROW, 2 * DFF], F32)
    fprm = sb("fprm_s", [128, 2 * DFF // 128 * FROW], F32)
    frow_in = sem("frow_in")
    fprm_t = sem("fprm_t")
    fprm_sb = sem("fprm_sb")
    fprm_out = sem("fprm_out")
    oh = sb("oh", [N_BUCKETS + 1, NU], F32)
    rel = sb("rel", [N_BUCKETS + 1, H], F32)
    bias_rows = sb("bias_rows", [H, NU], F32)
    lam = sb("lam", [1, 4, HD], F32)
    lprod = sb("lprod", [1, 2, HD], F32)
    lsum = sb("lsum", [1, 2], F32)
    lexp = sb("lexp", [1, 2], F32)
    ltmp = sb("ltmp", [1, 2], F32)
    ones_row = sb("ones_row", [1, 128], F32)
    sp_t = sb("sp_t", [128, 6, KT], F32)
    ps = c.ps
    prm_in = sem("prm_in")
    tab_in = sem("tab_in")
    lam_in = sem("lam_in")
    sub_in = sem("sub_in")
    id_zero = sem("id_zero")
    id_done = sem("id_done")
    fills = sem("fills")
    prm_t = sem("prm_t")
    prm_sb = sem("prm_sb")
    rows_mm = sem("rows_mm")
    rows_sb = sem("rows_sb")
    rows_out = sem("rows_out")
    tiles_out = sem("tiles_out")
    chain = sem("setup_chain")
    s_lsum = sem("s_lsum")
    s_lexp = sem("s_lexp")
    s_nl = sem("s_nl")
    s_nlb = sem("s_nlb")
    s_abs = sem("s_abs")
    s_e = sem("s_e")
    s_w = sem("s_w")
    s_ln = sem("s_ln")
    a_view = c.prm[:, :, ROW["rg_a_param"][0]]

    with nc.Block() as block:
        @block.sync
        def _(sp):
            for name in ("conv_w", "conv_b", "rg_b_a", "rg_b_x", "rg_a_param"):
                r, n = ROW[name]
                sp.dma_start(prow[r:r + n, :], flat(ins[name])).then_inc(prm_in, 16)
            r, n = ROW["h0"]
            sp.dma_start(prow[r:r + n, :], flat(ins["state_rglru_h"])).then_inc(prm_in, 16)
            r, n = ROW["conv_state"]
            sp.dma_start(prow[r:r + n, :], flat(ins["state_rglru_conv"])).then_inc(prm_in, 16)
            sp.dma_start(oh[:, :], ins["bucket_onehot"]).then_inc(tab_in, 16)
            sp.dma_start(rel[0:N_BUCKETS, :], ins["rel_bias"]).then_inc(tab_in, 16)
            for i, name in enumerate(("lambda_q1", "lambda_k1", "lambda_q2", "lambda_k2")):
                sp.dma_start(lam[:, i, :], ins[name]).then_inc(lam_in, 16)
            sp.dma_start(c.gsub[:, :], ins["subln_g"].rearrange("o p -> p o")).then_inc(sub_in, 16)
            sp.dma_start(frow[0:FCONV_W, :], flat(ins["ffn_conv_w"])).then_inc(frow_in, 16)
            sp.dma_start(frow[FCONV_W:FCONV_W + 1, :], flat(ins["ffn_conv_b"])).then_inc(frow_in, 16)
            sp.dma_start(frow[FCONV_W + 1:FROW, :], flat(ins["state_ffn_conv"])).then_inc(frow_in, 16)
            sp.wait_ge(rows_sb, 1)
            sp.dma_start(c.bias_rows_dram, bias_rows[:, :]).then_inc(rows_out, 16)
            sp.wait_ge(rows_out, 16)
            rows_t = c.bias_rows_dram.tensor
            sp.dma_start(c.bias_tiles_dram, bass.AP(tensor=rows_t, offset=U0 - (BW - 256),
                                                    ap=[[NU, H], [-1, 128], [1, BW]])).then_inc(tiles_out, 16)
            by_map = c.sbias_dram.rearrange("o (h m t) n -> m (o h) t n", h=H, m=2)
            for m in range(2):
                sp.dma_start(by_map[m], bass.AP(tensor=rows_t, offset=DEC_T - 1,
                                                ap=[[NU, H], [-1, DEC_T], [1, NKEYS]])).then_inc(tiles_out, 16)
            sp.wait_ge(fprm_sb, 1)
            sp.dma_start(c.fprm_dram, fprm[:, :]).then_inc(fprm_out, 16)
            sp.wait_ge(fprm_out, 16)
            sp.wait_ge(tiles_out, 16 * 3)

        @block.gpsimd
        def _(pool):
            pool.memset(c.ident[:, :], 0.0).then_inc(id_zero, 1)
            pool.wait_ge(id_zero, 1)
            pool.affine_select(out=c.ident[:, :], in_=c.ident[:, :], compare_op=ALU.not_equal, fill=1.0,
                               base=0, pattern=[[-1, 128]], channel_multiplier=1).then_inc(id_done, 1)

        @block.tensor
        def _(pe):
            pe.wait_ge(prm_in, 16 * 7)
            pe.wait_ge(id_done, 1)
            for k in range(KT):
                last = pe.transpose(ps[:, 0, NROW * k:NROW * (k + 1)], prow[:, 128 * k:128 * (k + 1)],
                                    c.ident[0:NROW, 0:NROW])
            last.then_inc(prm_t, 1)
            pe.wait_ge(tab_in, 32)
            pe.wait_ge(fills, 3)
            for i in range(3):
                last = pe.matmul(ps[0:H, 1 + i, 0:UW], rel[:, :], oh[:, UW * i:UW * (i + 1)],
                                 start=True, stop=True)
            last.then_inc(rows_mm, 1)
            pe.wait_ge(frow_in, 48)
            half = DFF // 128
            for k in range(2 * half):
                last = pe.transpose(ps[:, 5 + k // half, FROW * (k % half):FROW * (k % half + 1)],
                                    frow[:, 128 * k:128 * (k + 1)], c.ident[0:FROW, 0:FROW])
            last.then_inc(fprm_t, 1)
            pe.wait_ge(s_nl, 1)
            pe.matmul(ps[:, 4, 0:1], ones_row[:, :], ltmp[:, 1:2], start=True, stop=True).then_inc(s_nlb, 1)

        @block.scalar
        def _(act):
            act.wait_ge(s_lsum, 1)
            act.activation(lexp[:, :], lsum[:, :], ACT.Exp).then_inc(s_lexp, 1)
            act.wait_ge(s_abs, 1)
            act.activation(sp_t[:, 1, :], sp_t[:, 0, :], ACT.Exp, scale=-1.0).then_inc(s_e, 1)
            act.wait_ge(s_w, 1)
            act.activation(sp_t[:, 3, :], sp_t[:, 2, :], ACT.Ln).then_inc(s_ln, 1)

        @block.vector
        def _(dve):
            n = [0]

            def link(ins_):
                n[0] += 1
                ins_.then_inc(chain, 1)
                dve.wait_ge(chain, n[0])

            dve.memset(rel[N_BUCKETS:N_BUCKETS + 1, :], NEG).then_inc(fills, 1)
            dve.memset(ones_row[:, :], 1.0).then_inc(fills, 1)
            dve.memset(c.ones[:, :], 1.0).then_inc(fills, 1)
            dve.wait_ge(lam_in, 64)
            link(dve.tensor_tensor(lprod[:, :, :], lam[:, 0:4:2, :], lam[:, 1:4:2, :], ALU.mult))
            dve.reduce_sum(lsum[:, :], lprod[:, :, :], mybir.AxisListType.X).then_inc(s_lsum, 1)
            dve.wait_ge(s_lexp, 1)
            link(dve.tensor_tensor(ltmp[:, 0:1], lexp[:, 1:2], lexp[:, 0:1], ALU.subtract))
            dve.tensor_scalar(ltmp[:, 1:2], ltmp[:, 0:1], -LAMBDA_INIT, None, ALU.add).then_inc(s_nl, 1)
            dve.wait_ge(s_nlb, 1)
            dve.tensor_copy(c.neglam[:, :], ps[:, 4, 0:1])
            dve.wait_ge(sub_in, 16)
            dve.tensor_scalar(c.gsub[:, :], c.gsub[:, :], 1.0 - LAMBDA_INIT, None, ALU.mult)
            dve.wait_ge(fprm_t, 1)
            dve.tensor_copy(fprm[:, :].rearrange("p (a n) -> p a n", a=2), ps[:, 5:7, 0:DFF // 128 * FROW])\
               .then_inc(fprm_sb, 1)
            dve.wait_ge(rows_mm, 1)
            dve.tensor_copy(bias_rows[:, :].rearrange("h (i n) -> h i n", i=3), ps[0:H, 1:4, 0:UW])\
               .then_inc(rows_sb, 1)
            dve.wait_ge(prm_t, 1)
            link(dve.tensor_copy(c.prm[:, :, 0:NROW], ps[:, 0, 0:NROW * KT].rearrange("p (k r) -> p k r", k=KT)))
            link(dve.tensor_scalar(sp_t[:, 5, :], a_view, -1.0, None, ALU.mult))
            dve.tensor_tensor(sp_t[:, 0, :], sp_t[:, 5, :], a_view, ALU.max).then_inc(s_abs, 1)
            dve.wait_ge(s_e, 1)
            dve.tensor_scalar(sp_t[:, 2, :], sp_t[:, 1, :], 1.0, None, ALU.add).then_inc(s_w, 1)
            dve.wait_ge(s_ln, 1)
            link(dve.tensor_scalar(sp_t[:, 4, :], sp_t[:, 2, :], -1.0, None, ALU.add))
            link(dve.tensor_scalar(sp_t[:, 0, :], sp_t[:, 4, :], 0.0, None, ALU.is_equal))
            link(dve.tensor_scalar(sp_t[:, 4, :], sp_t[:, 4, :], 1e-30, None, ALU.max))
            link(dve.reciprocal(sp_t[:, 4, :], sp_t[:, 4, :]))
            link(dve.tensor_tensor(sp_t[:, 4, :], sp_t[:, 4, :], sp_t[:, 3, :], ALU.mult))
            link(dve.tensor_tensor(sp_t[:, 4, :], sp_t[:, 4, :], sp_t[:, 0, :], ALU.add))
            link(dve.tensor_tensor(sp_t[:, 4, :], sp_t[:, 4, :], sp_t[:, 1, :], ALU.mult))
            link(dve.tensor_scalar(sp_t[:, 5, :], sp_t[:, 5, :], 0.0, None, ALU.max))
            link(dve.tensor_tensor(sp_t[:, 4, :], sp_t[:, 4, :], sp_t[:, 5, :], ALU.add))
            dve.tensor_scalar(a_view, sp_t[:, 4, :], -RG_C, None, ALU.mult)
            dve.tensor_scalar(c.prm[:, :, NROW], sp_t[:, 4, :], RG_C, None, ALU.mult)


TURN = [
    ("P", K_, 0), ("W", Q_), ("P", K_, 1), ("P", K_, 2),
    ("P", Q_, 0), ("W", V_), ("TR", K_, 0), ("P", Q_, 1), ("TR", K_, 1), ("P", Q_, 2), ("TR", K_, 2),
    ("P", V_, 0), ("W", GA), ("P", V_, 1), ("TR", V_, 0), ("QK", 0), ("P", V_, 2), ("TR", V_, 1),
    ("P", GA, 0), ("W", XR), ("RW",), ("TW", 0, 0), ("TR", V_, 2), ("QK", 1),
    ("P", GA, 1), ("TW", 1, 0), ("QK", 2), ("PV", 0), ("P", GA, 2), ("TW", 2, 0), ("QK", 3), ("SS", 0),
    ("P", XR, 0), ("W", GB), ("TW", 3, 0), ("QK", 4), ("PV", 1),
    ("P", XR, 1), ("G", 0), ("SS", 1), ("TW", 4, 0), ("TW", 4, 1), ("QK", 5),
    ("P", XR, 2), ("G", 1), ("TW", 5, 0), ("TW", 5, 1), ("QK", 6), ("PV", 2),
    ("P", GB, 0), ("W", K_), ("G", 2), ("SS", 2), ("TW", 6, 0), ("TW", 6, 1), ("QK", 7),
    ("P", GB, 1), ("P", GB, 2), ("ST",), ("TW", 7, 0), ("TW", 7, 1), ("PV", 3), ("SS", 3), ("FG",),
]


def indices():
    ring, tbank = {}, {}
    for s in TURN:
        if s[0] == "P":
            ring[s] = len(ring)
        if s[0] == "G":
            ring[s + ("r",)] = len(ring)
            ring[s + ("i",)] = len(ring)
        if s[0] in ("TR", "TW", "ST"):
            tbank[s] = len(tbank)
    return ring, tbank


RING, TBANK = indices()
NRING, NTB = len(RING), len(TBANK)


def blocks_of(cc):
    off, n = CHUNKS[cc]
    return [(b, min(128, n - b), off + b >= SEQ) for b in range(0, n, 128)]


def heads(nc, sb, sem, ins, outs, c):
    ps = c.ps
    ring = [ps[:, 0, :], ps[:, 1, :]]
    S = [ps[:, 2:4, :].rearrange("p a n -> p (a n)"), ps[:, 4:6, :].rearrange("p a n -> p (a n)")]
    tb = ps[:, 6, :]
    ob = ps[:, 7, :]

    w_raw = sb("w_raw", [128, 3, KT, 128], F32)
    w_hi = sb("w_hi", [128, 2, KT, 128], F32R)
    w_lo = sb("w_lo", [128, 2, KT, 128], F32R)
    rg_raw = sb("rg_raw", [128, 2, 128], F32)
    rg_hi = sb("rg_hi", [128, 2, 128], F32R)
    rg_lo = sb("rg_lo", [128, 2, 128], F32R)
    q_hi = sb("q_hi", [128, SEQ], F32R)
    q_lo = sb("q_lo", [128, SEQ], F32R)
    k_hi = sb("k_hi", [128, SEQ], F32R)
    k_lo = sb("k_lo", [128, SEQ], F32R)
    kvf = sb("kvf", [128, 2, 384], F32)
    rows = sb("rows", [128, 2, 3, 128], F32)
    v_hi = sb("v_hi", [128, 8, 128], F32R)
    v_lo = sb("v_lo", [128, 8, 128], F32R)
    ga = sb("ga", [128, NTOK], F32)
    gb = sb("gb", [128, NTOK], F32)
    mg = sb("mg", [128, NTOK], F32)
    E = [sb("E0", [128, SEQ], F32), sb("E1", [128, SEQ], F32)]
    wt_hi = sb("wt_hi", [128, 8, 256], F32R)
    wt_lo = sb("wt_lo", [128, 8, 256], F32R)
    bias = sb("bias", [128, BW], F32)
    mx = sb("mx", [128, 2], F32)
    nmx = sb("nmx", [128, 2], F32)
    den = sb("den", [128, 2], F32)
    rden = sb("rden", [128, 3], F32)
    oT = sb("oT", [128, 256], F32)
    sq = sb("sq", [128, 256], F32)
    rst = sb("rst", [128, 256], F32)
    xe = sb("xe", [128, CONV_W - 1 + SEQ], F32)
    xs = sb("xs", [128, DEC_B, CONV_W - 1 + DEC_T], F32)
    hp = sb("hp", [128, NROW + 1], F32)
    xc = sb("xc", [128, 2, 384], F32)
    xc_hi = sb("xc_hi", [128, 2, 384], F32R)
    xc_lo = sb("xc_lo", [128, 2, 384], F32R)
    rr = sb("rr", [128, 384], F32)
    ii = sb("ii", [128, 384], F32)
    mt = sb("mt", [128, 384], F32)
    aa = sb("aa", [128, 384], F32)
    a2 = sb("a2", [128, 384], F32)
    yy = sb("yy", [128, 384], F32)
    carry = sb("carry", [128, 1], F32)
    tmp8 = sb("tmp8", [128, DEC_B], F32)
    NST = 1 + DEC_B + (CONV_W - 1) * (1 + DEC_B)
    stc = sb("stc", [128, NST], F32)
    st_rows = sb("st_rows", [NST, 128], F32)
    eps = sb("h_eps", [128, 1], F32)

    def par(name, k=0):
        i = ROW[name][0] + k
        return hp[:, i:i + 1]
    negc = hp[:, NROW:NROW + 1]

    raw_in = [sem(f"raw_in{u}") for u in range(3)]
    rg_in = sem("rg_in")
    bias_in = sem("bias_in")
    whi_done = sem("whi_done")
    wlo_done = sem("wlo_done")
    rghi_done = sem("rghi_done")
    rglo_done = sem("rglo_done")
    ring_done = sem("ring_done")
    ring_free = [sem("ring_free0"), sem("ring_free1")]
    t_done = sem("ht_done")
    t_free = sem("t_free")
    qk_done = sem("qk_done")
    ttr_done = sem("ttr_done")
    nmx_done = sem("nmx_done")
    exp_done = sem("exp_done")
    w_done = sem("w_done")
    wthi_done = sem("wthi_done")
    pv_done = sem("pv_done")
    sq_done = sem("sq_done")
    ss_done = sem("ss_done")
    rst_done = sem("rst_done")
    on_done = sem("on_done")
    khi_done = sem("khi_done")
    klo_done = sem("klo_done")
    qhi_done = sem("qhi_done")
    qlo_done = sem("qlo_done")
    vf_done = sem("vf_done")
    row_done = sem("row_done")
    vhi_done = sem("vhi_done")
    rows_out = [sem("rows_out0"), sem("rows_out1")]
    ga_done = sem("ga_done")
    gb_done = sem("gb_done")
    xr_done = sem("xr_done")
    hp_done = sem("hp_done")
    xc_done = sem("xc_done")
    xchi_done = sem("xchi_done")
    xclo_done = sem("xclo_done")
    r_done = sem("r_done")
    ta_done = sem("ta_done")
    m2_done = sem("m2_done")
    m_done = sem("m_done")
    y_done = sem("y_done")
    st_done = sem("st_done")
    pe_settled = sem("pe_settled")
    dve_settled = sem("dve_settled")
    str_done = sem("str_done")
    st_out = sem("st_out")
    mg_done = sem("mg_done")
    mg_out = sem("mg_out")
    setup_done = sem("heads_fill")
    dve_chain = sem("dve_chain")
    act_chain = sem("act_chain")
    DVE_LINKS, ACT_LINKS = c.links

    def cur(f, per, i):
        return per * f + per + i + 1

    def prev(f, per, i):
        return per * f + i + 1

    def now(f, per, i):
        return per * f + i + 1

    def ring_free_wait(eng, f, e):
        eng.wait_ge(ring_free[e % 2], NRING // 2 * f + NRING // 2 + e // 2)

    def turns(eng, body):
        with eng.Fori(0, H - 1) as f:
            body(f, False)
        body(H - 1, True)

    w_in = ins["w_in"].rearrange("o (k p) n -> p (o k) n", p=128)

    with nc.Block() as block:
        @block.sync
        def _(sp):
            k_rows = outs["k_rows_prompt"].rearrange("o b (t p) h n -> p (o b t) h n", p=128)
            v_rows = outs["v_rows_prompt"].rearrange("o b (t p) h n -> p (o b t) h n", p=128)
            k_new = outs["k_rows_sample"].rearrange("o b t h n -> (o b t) h n")
            v_new = outs["v_rows_sample"].rearrange("o b t h n -> (o b t) h n")

            def load_w(f, g):
                col = 128 * f + (COL0[g % 6] + 128 * (g // 6))
                sp.dma_start(w_raw[:, g % 3, :, :], w_in[:, :, bass.ds(col, 128)]).then_inc(raw_in[g % 3], 16)

            def body(f, last):
                sp.wait_ge(ttr_done, prev(f, 16, 15))
                sp.dma_start(bias[:, :], c.bias_tiles_dram[bass.ds(f, 1), :, :]
                             .rearrange("a p n -> p (a n)")).then_inc(bias_in, 16)
                sp.wait_ge(rglo_done, prev(f, 1, 0))
                for i, name in enumerate(("rg_w_a", "rg_w_x")):
                    sp.dma_start(rg_raw[:, i, :], ins[name][0, bass.ds(f, 1), :, :]
                                 .rearrange("a p n -> p (a n)")).then_inc(rg_in, 16)
                m = 0
                for s in TURN:
                    if s[0] == "W":
                        g = s[1] + (6 if s[1] == K_ else 0)
                        if not last or g + 3 < 6:
                            sp.wait_ge(wlo_done, cur(f, 6, g))
                            load_w(f, g + 3)
                    if s[0] == "TR":
                        big, new = (k_rows, k_new) if s[1] == K_ else (v_rows, v_new)
                        sp.wait_ge(row_done, now(f, 6, m))
                        b0 = CHUNKS[s[2]][0] // 128
                        nb = PROMPT_OF[s[2]] // 128
                        sp.dma_start(big[:, b0:b0 + nb, bass.ds(f, 1), :].rearrange("p t h n -> p t (h n)"),
                                     rows[:, m % 2, 0:nb, :]).then_inc(rows_out[m % 2], 16)
                        if s[2] == 2:
                            sp.dma_start(new[:, bass.ds(f, 1), :].rearrange("p h n -> p (h n)"),
                                         rows[0:NS, m % 2, 2, :]).then_inc(rows_out[m % 2], 16)
                        m += 1
                    if s[0] == "ST":
                        sp.wait_ge(str_done, now(f, 1, 0))
                        at = 0
                        for name, n in (("rglru_h_prompt", 1), ("rglru_h_sample", DEC_B),
                                        ("rglru_conv_prompt", 3), ("rglru_conv_sample", 3 * DEC_B)):
                            sp.dma_start(flat(outs[name])[:, bass.ds(128 * f, 128)], st_rows[at:at + n, :])\
                              .then_inc(st_out, 16)
                            at += n
                    if s[0] == "FG":
                        sp.wait_ge(mg_done, now(f, 1, 0))
                        sp.dma_start(c.merged_dram[bass.ds(f, 1), :, :].rearrange("a p n -> p (a n)"),
                                     mg[:, :]).then_inc(mg_out, 16)
            sp.sem_inc(mg_out, 16)
            sp.sem_inc(st_out, 64)
            for u in range(2):
                sp.sem_inc(rows_out[u], 64)
            for g in (K_, Q_, V_):
                load_w(0, g)
            sp.wait_ge(wlo_done, 7)
            load_w(0, GA)
            turns(sp, body)
            sp.wait_ge(mg_out, 16 * (H + 1))
            sp.wait_ge(st_out, 64 * (H + 1))
            for u in range(2):
                sp.wait_ge(rows_out[u], 64 * (H + 1))

        @block.scalar
        def _(act):
            act.sem_inc(whi_done, 6)
            act.sem_inc(rst_done, 4)
            act.wait_ge(setup_done, 2)

            def split_w(f, g, ahead):
                n = 6 * f + g + (6 if ahead else 0)
                act.wait_ge(raw_in[g % 3], 32 * f + 16 * (g // 3) + (48 if ahead else 16))
                gb2 = g - 2
                if gb2 >= 0:
                    act.wait_ge(ring_done, cur(f, NRING, RING[("P", gb2, 2)]))
                elif ahead:
                    act.wait_ge(ring_done, cur(f, NRING, RING[("P", gb2 + 6, 2)]))
                else:
                    act.wait_ge(ring_done, prev(f, NRING, RING[("P", gb2 + 6, 2)]))
                act.activation(w_hi[:, g % 2, :, :], w_raw[:, g % 3, :, :], ACT.Copy).then_inc(whi_done, 1)

            split_w(0, K_, False)

            def body(f, last):
                chain = [0]

                def link(ins_):
                    chain[0] += 1
                    ins_.then_inc(act_chain, 1)
                    act.wait_ge(act_chain, ACT_LINKS * f + chain[0])

                m = 0
                for s in TURN:
                    if s[0] == "W" and not (last and s[1] == K_):
                        split_w(f, s[1], s[1] == K_)
                    elif s[0] == "RW":
                        act.wait_ge(rg_in, 32 * f + 32)
                        act.wait_ge(ring_done, prev(f, NRING, RING[("G", 2, "i")]))
                        act.activation(rg_hi[:, :, :], rg_raw[:, :, :], ACT.Copy).then_inc(rghi_done, 1)
                    elif s[0] == "P":
                        g, cc = s[1:]
                        off, n = CHUNKS[cc]
                        np_ = PROMPT_OF[cc]
                        e = RING[s]
                        src = ring[e % 2]
                        act.wait_ge(ring_done, cur(f, NRING, e))
                        if g == K_:
                            if cc == 0:
                                act.wait_ge(ttr_done, prev(f, 16, 15))
                            act.activation(k_hi[:, off:off + np_], src[:, 0:np_], ACT.Copy).then_inc(khi_done, 1)
                        elif g == Q_:
                            act.activation(q_hi[:, off:off + np_], src[:, 0:np_], ACT.Copy,
                                           scale=HD ** -0.5).then_inc(qhi_done, 1)
                        elif g == V_:
                            act.wait_ge(t_done, cur(f, NTB, TBANK[("TR", K_, cc + 1)] if cc < 2
                                                    else TBANK[("TR", V_, 0)]))
                            act.activation(kvf[:, (3 + cc) % 2, 0:n], src[:, 0:n], ACT.Copy).then_inc(vf_done, 1)
                            act.wait_ge(vf_done, now(f, 3, cc))
                            act.sem_inc(ring_free[e % 2], 1)
                        elif g == XR:
                            if cc == 0:
                                act.wait_ge(y_done, prev(f, 3, 2))
                                act.wait_ge(st_done, prev(f, 1, 0))
                                act.wait_ge(hp_done, 2 * f + 2)
                            base = CONV_W - 1 + off
                            if cc == 2:
                                link(act.activation(
                                    xs[:, :, CONV_W - 1:], src[:, np_:n].rearrange("p (b t) -> p b t", b=DEC_B),
                                    ACT.Copy))
                            act.activation(xe[:, base:base + np_], src[:, 0:np_], ACT.Copy).then_inc(xr_done, 1)
                            act.wait_ge(xr_done, now(f, 3, cc))
                            act.sem_inc(ring_free[e % 2], 1)
                        elif g == GA:
                            if cc == 0:
                                act.wait_ge(mg_out, 16 * f + 16)
                            act.activation(ga[:, off:off + n], src[:, 0:n], ACT.Sigmoid).then_inc(ga_done, 1)
                            act.wait_ge(ga_done, now(f, 3, cc))
                            act.sem_inc(ring_free[e % 2], 1)
                        elif g == GB:
                            act.activation(gb[:, off:off + n], src[:, 0:n], ACT.Sigmoid).then_inc(gb_done, 1)
                            act.wait_ge(gb_done, now(f, 3, cc))
                            act.sem_inc(ring_free[e % 2], 1)
                        if g == XR:
                            act.wait_ge(xc_done, now(f, 3, cc))
                            act.wait_ge(ring_done, cur(f, NRING, RING[("G", 0, "i")]) if cc == 2
                                        else prev(f, NRING, RING[("G", 2, "i")]))
                            act.activation(xc_hi[:, cc % 2, 0:n], xc[:, cc % 2, 0:n], ACT.Copy).then_inc(xchi_done, 1)
                    elif s[0] == "G":
                        cc = s[1]
                        off, n = CHUNKS[cc]
                        for part, dst, name in (("r", rr, "rg_b_a"), ("i", ii, "rg_b_x")):
                            e = RING[s + (part,)]
                            act.wait_ge(ring_done, cur(f, NRING, e))
                            if part == "r":
                                act.wait_ge(y_done, prev(f, 3, 2) if cc == 0 else cur(f, 3, cc - 1))
                            act.activation(dst[:, 0:n], ring[e % 2][:, 0:n], ACT.Sigmoid,
                                           bias=par(name)).then_inc(r_done, 1)
                            act.wait_ge(r_done, 6 * f + 2 * cc + (1 if part == "r" else 2))
                            act.sem_inc(ring_free[e % 2], 1)
                        act.activation(mt[:, 0:n], rr[:, 0:n], ACT.Tanh, scale=negc)
                        link(act.activation(aa[:, 0:n], rr[:, 0:n], ACT.Exp, scale=par("rg_a_param")))
                        act.activation(a2[:, 0:n], aa[:, 0:n], ACT.Square).then_inc(ta_done, 1)
                        act.wait_ge(m2_done, now(f, 3, cc))
                        act.activation(mt[:, 0:n], a2[:, 0:n], ACT.Sqrt).then_inc(m_done, 1)
                    elif s[0] == "TR":
                        g, cc = s[1:]
                        act.wait_ge(t_done, cur(f, NTB, TBANK[s]))
                        before = {0: [0, 1, 3], 1: [0, 1, 2]}[m % 2][m // 2]
                        act.wait_ge(rows_out[m % 2], 64 * f + 64 + 16 * before)
                        nb = PROMPT_OF[cc] // 128
                        if cc == 2:
                            link(act.activation(rows[0:NS, m % 2, 2, :], tb[0:NS, 256:384], ACT.Copy))
                        act.activation(rows[:, m % 2, 0:nb, :],
                                       tb[:, 0:128 * nb].rearrange("p (b n) -> p b n", b=nb),
                                       ACT.Copy).then_inc(row_done, 1)
                        if g == V_:
                            if cc == 0:
                                act.wait_ge(pv_done, prev(f, 4, 3))
                            b0 = CHUNKS[cc][0] // 128
                            act.activation(v_hi[:, b0:b0 + nb, :],
                                           tb[:, 0:128 * nb].rearrange("p (b n) -> p b n", b=nb),
                                           ACT.Copy).then_inc(vhi_done, 1)
                        else:
                            act.wait_ge(row_done, now(f, 6, m))
                            act.sem_inc(t_free, 1)
                        m += 1
                    elif s[0] == "ST":
                        act.wait_ge(t_done, cur(f, NTB, TBANK[s]))
                        act.wait_ge(st_out, 64 * f + 64)
                        act.activation(st_rows[:, :], tb[0:NST, 0:128], ACT.Copy).then_inc(str_done, 1)
                        act.wait_ge(str_done, now(f, 1, 0))
                        act.sem_inc(t_free, 1)
                    elif s[0] == "QK":
                        j = s[1]
                        n = 256 * (j // 2 + 1)
                        act.wait_ge(nmx_done, now(f, 8, j))
                        for i in range(2):
                            act.activation(E[i][:, 0:n], E[i][:, 0:n], ACT.Exp, bias=nmx[:, i:i + 1],
                                           accum_out=den[:, i:i + 1]).then_inc(exp_done, 1)
                    elif s[0] == "TW":
                        j, part = s[1:]
                        nb = min(4, 2 * (j // 2 + 1) - 4 * part)
                        act.wait_ge(t_done, cur(f, NTB, TBANK[s]))
                        if j % 2 == 0 and part == 0:
                            p = j // 2
                            act.wait_ge(pv_done, prev(f, 4, 3) if p == 0 else cur(f, 4, p - 1))
                        act.activation(wt_hi[:, 4 * part:4 * part + nb, 128 * (j % 2):128 * (j % 2) + 128],
                                       tb[:, 0:128 * nb].rearrange("p (b n) -> p b n", b=nb),
                                       ACT.Copy).then_inc(wthi_done, 1)
                    elif s[0] == "PV":
                        p = s[1]
                        act.wait_ge(pv_done, cur(f, 4, p))
                        act.wait_ge(on_done, prev(f, 4, 3) if p == 0 else cur(f, 4, p - 1))
                        act.activation(sq[:, :], ob[:, 0:256], ACT.Square)
                        act.activation(oT[:, :], ob[:, 0:256], ACT.Copy).then_inc(sq_done, 1)
                    elif s[0] == "SS":
                        p = s[1]
                        act.wait_ge(ss_done, now(f, 4, p))
                        link(act.activation(rst[:, :], ob[:, 256:512], ACT.Ln, bias=eps[:, :], scale=1.0 / KV))
                        act.activation(rst[:, :], rst[:, :], ACT.Exp, scale=-0.5).then_inc(rst_done, 1)
                assert chain[0] == ACT_LINKS, ("ACT_LINKS", chain[0])
            turns(act, body)

        @block.vector
        def _(dve):
            dve.memset(eps[:, :], EPS).then_inc(setup_done, 1)
            dve.memset(xe[:, 0:CONV_W - 1], 0.0).then_inc(setup_done, 1)
            dve.sem_inc(wlo_done, 6)
            dve.sem_inc(rglo_done, 1)
            dve.sem_inc(t_free, NTB)
            dve.sem_inc(ttr_done, 16)
            dve.sem_inc(on_done, 4)
            dve.sem_inc(xclo_done, 3)
            dve.sem_inc(y_done, 3)
            dve.sem_inc(st_done, 1)
            for u in range(2):
                dve.sem_inc(ring_free[u], NRING // 2)

            def split_w(f, g, ahead):
                dve.wait_ge(whi_done, 6 * f + g + (13 if ahead else 7))
                dve.tensor_tensor(w_lo[:, g % 2, :, :], w_raw[:, g % 3, :, :],
                                  w_hi[:, g % 2, :, :].bitcast(F32), ALU.subtract).then_inc(wlo_done, 1)

            split_w(0, K_, False)

            def body(f, last):
                chain = [0]

                def link(ins_):
                    chain[0] += 1
                    ins_.then_inc(dve_chain, 1)
                    dve.wait_ge(dve_chain, DVE_LINKS * f + chain[0])

                m = 0
                for s in TURN:
                    if s[0] == "W" and not (last and s[1] == K_):
                        split_w(f, s[1], s[1] == K_)
                    elif s[0] == "RW":
                        dve.wait_ge(rghi_done, now(f, 1, 0))
                        dve.tensor_tensor(rg_lo[:, :, :], rg_raw[:, :, :], rg_hi[:, :, :].bitcast(F32),
                                          ALU.subtract).then_inc(rglo_done, 1)
                        dve.tensor_copy(hp[:, :], c.prm[:, bass.ds(f, 1), :].rearrange("p a n -> p (a n)"))\
                           .then_inc(hp_done, 1)
                        dve.wait_ge(hp_done, 2 * f + 1)
                        r0 = ROW["conv_state"][0]
                        dve.tensor_copy(xs[:, :, 0:CONV_W - 1], hp[:, r0:r0 + 3 * DEC_B]
                                        .rearrange("p (b t) -> p b t", b=DEC_B)).then_inc(hp_done, 1)
                    elif s[0] == "P" and s[1] in (K_, Q_):
                        g, cc = s[1:]
                        off, n = CHUNKS[cc]
                        np_ = PROMPT_OF[cc]
                        e = RING[s]
                        src = ring[e % 2]
                        if g == K_:
                            dve.wait_ge(khi_done, now(f, 3, cc))
                            if cc == 0:
                                dve.wait_ge(t_done, prev(f, NTB, TBANK[("TR", V_, 1)]))
                            elif cc == 1:
                                dve.wait_ge(t_done, prev(f, NTB, TBANK[("TR", V_, 2)]))
                            else:
                                dve.wait_ge(t_done, cur(f, NTB, TBANK[("TR", K_, 0)]))
                            if cc == 2:
                                dve.tensor_copy(c.k_new[:, bass.ds(f, 1), :].rearrange("p a n -> p (a n)"),
                                                src[:, np_:n])
                            dve.tensor_copy(kvf[:, cc % 2, 0:n], src[:, 0:n])
                            dve.tensor_tensor(k_lo[:, off:off + np_], src[:, 0:np_],
                                              k_hi[:, off:off + np_].bitcast(F32), ALU.subtract)\
                               .then_inc(klo_done, 1)
                            dve.wait_ge(klo_done, now(f, 3, cc))
                        else:
                            dve.wait_ge(qhi_done, now(f, 3, cc))
                            if cc == 2:
                                dve.tensor_scalar(c.q_new[:, bass.ds(f, 1), :].rearrange("p a n -> p (a n)"),
                                                  src[:, np_:n], HD ** -0.5, None, ALU.mult)
                            dve.scalar_tensor_tensor(out=q_lo[:, off:off + np_], in0=src[:, 0:np_],
                                                     scalar=HD ** -0.5, in1=q_hi[:, off:off + np_].bitcast(F32),
                                                     op0=ALU.mult, op1=ALU.subtract).then_inc(qlo_done, 1)
                            dve.wait_ge(qlo_done, now(f, 3, cc))
                        dve.sem_inc(ring_free[e % 2], 1)
                    elif s[0] == "P" and s[1] == XR:
                        cc = s[2]
                        off, n = CHUNKS[cc]
                        np_ = PROMPT_OF[cc]
                        dve.wait_ge(xr_done, now(f, 3, cc))
                        prompt = [xe[:, off + k:off + k + np_] for k in range(CONV_W)]
                        link(dve.tensor_scalar(xc[:, cc % 2, 0:np_], prompt[0], par("conv_w", 0), par("conv_b"),
                                               ALU.mult, ALU.add))
                        for k in range(1, CONV_W):
                            ins_ = dve.scalar_tensor_tensor(out=xc[:, cc % 2, 0:np_], in0=prompt[k], scalar=par("conv_w", k),
                                                            in1=xc[:, cc % 2, 0:np_], op0=ALU.mult, op1=ALU.add)
                            if k < CONV_W - 1 or cc == 2:
                                link(ins_)
                        if cc == 2:
                            samp = xc[:, cc % 2, np_:n].rearrange("p (b t) -> p b t", b=DEC_B)
                            link(dve.tensor_scalar(samp, xs[:, :, 0:DEC_T], par("conv_w", 0), par("conv_b"),
                                                   ALU.mult, ALU.add))
                            for k in range(1, CONV_W):
                                ins_ = dve.scalar_tensor_tensor(out=samp, in0=xs[:, :, k:k + DEC_T],
                                                                scalar=par("conv_w", k), in1=samp,
                                                                op0=ALU.mult, op1=ALU.add)
                                if k < CONV_W - 1:
                                    link(ins_)
                        ins_.then_inc(xc_done, 1)
                        dve.wait_ge(xchi_done, now(f, 3, cc))
                        dve.tensor_tensor(xc_lo[:, cc % 2, 0:n], xc[:, cc % 2, 0:n],
                                          xc_hi[:, cc % 2, 0:n].bitcast(F32), ALU.subtract)\
                           .then_inc(xclo_done, 1)
                    elif s[0] == "G":
                        cc = s[1]
                        off, n = CHUNKS[cc]
                        np_ = PROMPT_OF[cc]
                        dve.wait_ge(ta_done, now(f, 3, cc))
                        dve.scalar_tensor_tensor(out=a2[:, 0:n], in0=a2[:, 0:n], scalar=1.0, in1=mt[:, 0:n],
                                                 op0=ALU.add, op1=ALU.mult).then_inc(m2_done, 1)
                        dve.wait_ge(m_done, now(f, 3, cc))
                        if cc == 0:
                            link(dve.memset(mt[:, 0:1], 1.0))
                            link(dve.memset(aa[:, 0:1], 0.0))
                        link(dve.tensor_tensor(ii[:, 0:n], ii[:, 0:n], mt[:, 0:n], ALU.mult))
                        link(dve.tensor_tensor(ii[:, 0:n], ii[:, 0:n], xc[:, cc % 2, 0:n], ALU.mult))
                        if cc == 2:
                            a_s = aa[:, np_:n].rearrange("p (b t) -> p b t", b=DEC_B)[:, :, 0]
                            b_s = ii[:, np_:n].rearrange("p (b t) -> p b t", b=DEC_B)[:, :, 0]
                            h0 = hp[:, ROW["h0"][0]:ROW["h0"][0] + DEC_B]
                            link(dve.tensor_tensor(tmp8[:, :], a_s, h0, ALU.mult))
                            link(dve.tensor_tensor(b_s, b_s, tmp8[:, :], ALU.add))
                            link(dve.memset(a_s, 0.0))
                        link(dve.tensor_tensor_scan(yy[:, 0:n], aa[:, 0:n], ii[:, 0:n],
                                                    0.0 if cc == 0 else carry[:, :], ALU.mult, ALU.add))
                        if cc < 2:
                            link(dve.tensor_copy(carry[:, :], yy[:, n - 1:n]))
                        else:
                            link(dve.tensor_copy(stc[:, 0:1], yy[:, np_ - 1:np_]))
                            link(dve.tensor_copy(stc[:, 1:1 + DEC_B], yy[:, np_:n]
                                                 .rearrange("p (b t) -> p b t", b=DEC_B)[:, :, DEC_T - 1]))
                            at = 1 + DEC_B
                            link(dve.tensor_copy(stc[:, at:at + 3], xe[:, SEQ:SEQ + 3]))
                            dve.tensor_copy(stc[:, at + 3:NST].rearrange("p (b t) -> p b t", b=DEC_B),
                                            xs[:, :, DEC_T:DEC_T + 3]).then_inc(st_done, 1)
                        dve.wait_ge(ga_done, now(f, 3, cc))
                        dve.tensor_tensor(ga[:, off:off + n], ga[:, off:off + n], yy[:, 0:n], ALU.mult)\
                           .then_inc(y_done, 1)
                    elif s[0] == "TR" and s[1] == V_:
                        cc = s[2]
                        nb = PROMPT_OF[cc] // 128
                        b0 = CHUNKS[cc][0] // 128
                        dve.wait_ge(vhi_done, now(f, 3, cc))
                        dve.tensor_tensor(v_lo[:, b0:b0 + nb, :],
                                          tb[:, 0:128 * nb].rearrange("p (b n) -> p b n", b=nb),
                                          v_hi[:, b0:b0 + nb, :].bitcast(F32), ALU.subtract).then_inc(t_free, 1)
                    elif s[0] == "QK":
                        j = s[1]
                        n = 256 * (j // 2 + 1)
                        c0 = BW - 256 - 128 * j
                        if j == 0:
                            dve.wait_ge(bias_in, 16 * f + 16)
                        dve.wait_ge(qk_done, now(f, 8, j))
                        if j == 0:
                            dve.wait_ge(t_done, prev(f, NTB, TBANK[("TW", 7, 1)]))
                        else:
                            q = 1 if ("TW", j - 1, 1) in TBANK else 0
                            dve.wait_ge(t_done, cur(f, NTB, TBANK[("TW", j - 1, q)]))
                        dve.sem_inc(dve_settled, 1)
                        for i in range(2):
                            dve.tensor_tensor_reduce(out=E[i][:, 0:n], in0=S[i][:, 0:n], in1=bias[:, c0:c0 + n],
                                                     scale=1.0, scalar=-3e38, op0=ALU.add, op1=ALU.max,
                                                     accum_out=mx[:, i:i + 1]).then_inc(ttr_done, 1)
                        dve.wait_ge(ttr_done, cur(f, 16, 2 * j + 1))
                        dve.tensor_scalar(nmx[:, :], mx[:, :], -1.0, None, ALU.mult).then_inc(nmx_done, 1)
                        dve.wait_ge(exp_done, now(f, 16, 2 * j + 1))
                        link(dve.reciprocal(rden[:, 0:2], den[:, :]))
                        link(dve.tensor_tensor(rden[:, 2:3], rden[:, 1:2], c.neglam[:, :], ALU.mult))
                        link(dve.tensor_scalar(E[1][:, 0:n], E[1][:, 0:n], rden[:, 2:3], None, ALU.mult))
                        dve.scalar_tensor_tensor(out=E[0][:, 0:n], in0=E[0][:, 0:n], scalar=rden[:, 0:1],
                                                 in1=E[1][:, 0:n], op0=ALU.mult, op1=ALU.add).then_inc(w_done, 1)
                        dve.wait_ge(w_done, now(f, 8, j))
                    elif s[0] == "TW":
                        j, part = s[1:]
                        nb = min(4, 2 * (j // 2 + 1) - 4 * part)
                        dst = (slice(None), slice(4 * part, 4 * part + nb), slice(128 * (j % 2), 128 * (j % 2) + 128))
                        dve.wait_ge(wthi_done, 12 * f + [x for x in TURN if x[0] == "TW"].index(s) + 1)
                        dve.tensor_tensor(wt_lo[dst], tb[:, 0:128 * nb].rearrange("p (b n) -> p b n", b=nb),
                                          wt_hi[dst].bitcast(F32), ALU.subtract).then_inc(t_free, 1)
                    elif s[0] == "SS":
                        p = s[1]
                        dve.wait_ge(rst_done, cur(f, 4, p))
                        if p == 0:
                            dve.wait_ge(mg_out, 16 * f + 16)
                        dve.scalar_tensor_tensor(out=mg[:, 256 * p:256 * (p + 1)], in0=oT[:, :], scalar=c.gsub[:, :],
                                                 in1=rst[:, :], op0=ALU.mult, op1=ALU.mult).then_inc(on_done, 1)
                    elif s[0] == "FG":
                        dve.wait_ge(gb_done, now(f, 3, 2))
                        dve.wait_ge(on_done, cur(f, 4, 3))
                        dve.wait_ge(y_done, cur(f, 3, 2))
                        link(dve.tensor_tensor(mg[:, 0:SEQ], mg[:, 0:SEQ], gb[:, 0:SEQ], ALU.mult))
                        link(dve.tensor_tensor(mg[:, 0:SEQ], mg[:, 0:SEQ], ga[:, 0:SEQ], ALU.add))
                        link(dve.tensor_copy(c.gb_new[:, bass.ds(f, 1), :].rearrange("p a n -> p (a n)"),
                                             gb[:, SEQ:NTOK]))
                        dve.tensor_copy(mg[:, SEQ:NTOK], ga[:, SEQ:NTOK]).then_inc(mg_done, 1)
                assert chain[0] == DVE_LINKS, ("DVE_LINKS", chain[0])
            turns(dve, body)

        @block.tensor
        def _(pe):
            pe.sem_inc(ring_done, NRING)
            pe.sem_inc(t_done, NTB)
            pe.sem_inc(pv_done, 4)

            def body(f, last):
                for s in TURN:
                    if s[0] == "P":
                        g, cc = s[1:]
                        off, n = CHUNKS[cc]
                        e = RING[s]
                        if cc == 0:
                            pe.wait_ge(wlo_done, cur(f, 6, g))
                        ring_free_wait(pe, f, e)
                        for k in range(KT):
                            for i, (w, x) in enumerate(((w_hi, c.h_hi), (w_hi, c.h_lo), (w_lo, c.h_hi))):
                                last_ = pe.matmul(ring[e % 2][:, 0:n], w[:, g % 2, k, :], x[:, k, off:off + n],
                                                  start=(k == 0 and i == 0), stop=(k == KT - 1 and i == 2))
                        last_.then_inc(ring_done, 1)
                    elif s[0] == "G":
                        cc = s[1]
                        off, n = CHUNKS[cc]
                        pe.wait_ge(xclo_done, cur(f, 3, cc))
                        if cc == 0:
                            pe.wait_ge(rglo_done, cur(f, 1, 0))
                        for gi, part in enumerate(("r", "i")):
                            e = RING[s + (part,)]
                            ring_free_wait(pe, f, e)
                            for i, (w, x) in enumerate(((rg_hi, xc_hi), (rg_hi, xc_lo), (rg_lo, xc_hi))):
                                last_ = pe.matmul(ring[e % 2][:, 0:n], w[:, gi, :], x[:, cc % 2, 0:n],
                                                  start=(i == 0), stop=(i == 2))
                            last_.then_inc(ring_done, 1)
                    elif s[0] == "TR":
                        g, cc = s[1:]
                        if g == K_:
                            pe.wait_ge(klo_done, now(f, 3, cc))
                        else:
                            pe.wait_ge(vf_done, now(f, 3, cc))
                        pe.wait_ge(t_free, NTB * f + NTB + TBANK[s])
                        slot = (cc if g == K_ else 3 + cc) % 2
                        for b, n, _ in blocks_of(cc):
                            last_ = pe.transpose(tb[0:n, b:b + 128], kvf[:, slot, b:b + n], c.ident[:, :])
                        last_.then_inc(t_done, 1)
                    elif s[0] == "ST":
                        pe.wait_ge(st_done, cur(f, 1, 0))
                        pe.wait_ge(t_free, NTB * f + NTB + TBANK[s])
                        pe.sem_inc(pe_settled, 1)
                        pe.transpose(tb[0:NST, 0:128], stc[:, :], c.ident[:, :]).then_inc(t_done, 1)
                    elif s[0] == "QK":
                        j = s[1]
                        nk = 256 * (j // 2 + 1)
                        if j == 0:
                            pe.wait_ge(klo_done, now(f, 3, 2))
                            pe.wait_ge(qlo_done, now(f, 3, 2))
                        pe.wait_ge(ttr_done, prev(f, 16, 15) if j == 0 else cur(f, 16, 2 * j - 1))
                        for i in range(2):
                            part = slice(64 * i, 64 * i + 64)
                            for k0 in range(0, nk, 512):
                                n = min(512, nk - k0)
                                for x, (a, b) in enumerate(((q_hi, k_hi), (q_hi, k_lo), (q_lo, k_hi))):
                                    last_ = pe.matmul(S[i][:, k0:k0 + n], a[part, 128 * j:128 * (j + 1)],
                                                      b[part, k0:k0 + n], start=(x == 0), stop=(x == 2))
                        last_.then_inc(qk_done, 1)
                    elif s[0] == "TW":
                        j, part = s[1:]
                        nb = min(4, 2 * (j // 2 + 1) - 4 * part)
                        pe.wait_ge(w_done, now(f, 8, j))
                        pe.wait_ge(t_free, NTB * f + NTB + TBANK[s])
                        for b in range(nb):
                            kb = 4 * part + b
                            last_ = pe.transpose(tb[:, 128 * b:128 * (b + 1)], E[0][:, 128 * kb:128 * (kb + 1)],
                                                 c.ident[:, :])
                        last_.then_inc(t_done, 1)
                    elif s[0] == "PV":
                        p = s[1]
                        t_last = ("TW", 2 * p + 1, 1 if p >= 2 else 0)
                        pe.wait_ge(t_free, cur(f, NTB, TBANK[t_last]))
                        pe.wait_ge(rst_done, prev(f, 4, 3) if p == 0 else cur(f, 4, p - 1))
                        nkb = 2 * (p + 1)
                        for kb in range(nkb):
                            for i, (v, w) in enumerate(((v_hi, wt_hi), (v_lo, wt_hi), (v_hi, wt_lo))):
                                last_ = pe.matmul(ob[:, 0:256], v[:, kb, :], w[:, kb, :],
                                                  start=(kb == 0 and i == 0), stop=(kb == nkb - 1 and i == 2))
                        last_.then_inc(pv_done, 1)
                    elif s[0] == "SS":
                        p = s[1]
                        pe.wait_ge(sq_done, now(f, 4, p))
                        pe.matmul(ob[:, 256:512], c.ones[:, :], sq[:, :], start=True, stop=True).then_inc(ss_done, 1)
            turns(pe, body)


SC = NKEYS // 3


def pair_select():
    row = np.arange(128)
    head, m, t = row // 16, row // 8 % 2, row % 8
    sel = (np.arange(NS)[None, :] == (head * DEC_T + t)[:, None]).astype(np.float32)
    return np.concatenate([sel, m[:, None].astype(np.float32)], 1)


def sampled(nc, sb, sem, ins, outs, c):
    ps = c.ps
    S3 = ps[:, 0:3, 0:SC]
    ptn = ps[0:DEC_T, 6, 0:NS]
    tb = [ps[:, 3, :], ps[:, 4, :]]
    pt = ps[:, 5, :]
    o2 = ps[0:NS, 6:8, :].rearrange("p a n -> p (a n)")

    ptab = sb("ptab", [1, DEC_B * NPAGES], I32)
    sel = sb("sel", [128, NS + 1], F32)
    sgn = sb("sgn", [128, 2], F32)
    k_raw = sb("k_raw", [128, 2, NPAGES, D], F32)
    v_raw = sb("v_raw", [128, 2, D], F32)
    vn_raw = sb("vn_raw", [DEC_T, D], F32)
    v_hi = sb("sv_hi", [128, NPAGES, D], F32R)
    v_lo = sb("sv_lo", [128, NPAGES, D], F32R)
    vn_hi = sb("vn_hi", [DEC_T, D], F32R)
    vn_lo = sb("vn_lo", [DEC_T, D], F32R)
    kt_hi = sb("kt_hi", [128, 2, NKEYS], F32R)
    kt_lo = sb("kt_lo", [128, 2, NKEYS], F32R)
    qd_hi = sb("qd_hi", [128, H * 144], F32R)
    qd_lo = sb("qd_lo", [128, H * 144], F32R)
    sbias = sb("sbias", [128, NKEYS], F32)
    P = sb("P", [128, NKEYS], F32)
    mx = sb("s_mx", [128, 4], F32)
    C = sb("C", [128, NS], F32)
    pt_hi = sb("pt_hi", [128, NPAGES + 1, NS], F32R)
    pt_lo = sb("pt_lo", [128, NPAGES + 1, NS], F32R)
    o2s = sb("o2s", [NS, D], F32)
    oT = sb("s_oT", [128, H, NS], F32)
    mg = sb("s_mg", [128, H, NS], F32)
    eps = sb("s_eps", [128, 1], F32)

    tab_in = sem("ptab_in")
    const_in = sem("s_const_in")
    k_in = [sem("k_in0"), sem("k_in1")]
    v_in = [sem(f"v_in{u}") for u in range(2)]
    vn_in = sem("vn_in")
    ga_in = sem("ga_in")
    s_fill = sem("s_fill")
    tk_done = sem("tk_done")
    kthi_done = sem("kthi_done")
    ktlo_done = sem("ktlo_done")
    ktn_hi = sem("ktn_hi")
    ktn_lo = sem("ktn_lo")
    qdhi_done = sem("qdhi_done")
    qdlo_done = sem("qdlo_done")
    qkh_done = sem("qkh_done")
    ttr_done = sem("s_ttr_done")
    nmx_done = sem("s_nmx_done")
    exp_done = sem("s_exp_done")
    c_done = sem("c_done")
    vhi_done = sem("s_vhi_done")
    vlo_done = sem("s_vlo_done")
    vnhi_done = sem("vnhi_done")
    vnlo_done = sem("vnlo_done")
    pt_done = sem("pt_done")
    pthi_done = sem("pthi_done")
    ptlo_done = sem("ptlo_done")
    pv_done = sem("s_pv_done")
    o2_done = sem("o2_done")
    ot_done = sem("ot_done")
    ots_done = sem("ots_done")
    sq_done = sem("s_sq_done")
    ss_done = sem("s_ss_done")
    rst_done = sem("s_rst_done")
    mgn_done = sem("mgn_done")
    mgn_out = sem("mgn_out")
    pe_settled = sem("s_pe_settled")
    dve_settled = sem("s_dve_settled")
    chain = sem("s_chain")
    achain = sem("s_achain")

    def all_turns(eng, body):
        body(0, 0)
        body(1, 1)
        with eng.Fori(1, 3) as i:
            for u in range(2):
                body(2 * i + u, u)
        for b in range(6, DEC_B + 2):
            body(b, b % 2)

    def has(b, d):
        return not isinstance(b, int) or 0 <= b - d < DEC_B

    with nc.Block() as block:
        @block.sync
        def _(sp):
            sp.dma_start(ptab[:, :], ins["page_table"].rearrange("(o b) n -> o (b n)", o=1)).then_inc(tab_in, 16)
            sp.dma_start(sel[:, :], ins["pair_select"]).then_inc(const_in, 16)
            sp.dma_start(sbias[:, :], c.sbias_dram.rearrange("a p n -> p (a n)")).then_inc(const_in, 16)
            sp.dma_start(mg[:, :, :], c.merged_dram[:, :, SEQ:NTOK].rearrange("h p n -> p h n")).then_inc(ga_in, 16)
            sp.wait_ge(tab_in, 16)

            def page_of(b, n):
                return sp.value_load(ptab[0:1, bass.ds(NPAGES * b + n, 1)], min_val=0,
                                     max_val=ins["cache_k"].shape[1] - 1)

            def load(page, pool, dst, done):
                sp.dma_start(dst, pool[0, bass.ds(page, 1), :, :, :].rearrange("a p h n -> p (a h n)"))\
                  .then_inc(done, 16)

            def load_k(b, u, used=None):
                for n in range(NPAGES):
                    page = page_of(b, n)
                    if n == 0 and used is not None:
                        sp.wait_ge(tk_done, used)
                    load(page, ins["cache_k"], k_raw[:, u, n, :], k_in[u])

            load_k(0, 0)
            v_new = outs["v_rows_sample"].rearrange("o b t h n -> (o b t) (h n)")

            def body(b, u):
                if has(b, 1):
                    bv = b - 1

                    def load_v(lo, hi):
                        for n in range(lo, hi):
                            page = page_of(bv, n)
                            if not (isinstance(b, int) and bv == 0 and n < 2):
                                sp.wait_ge(vlo_done, 8 * bv + n - 1)
                            load(page, ins["cache_v"], v_raw[:, n % 2, :], v_in[n % 2])
                    load_v(0, 2)
                    if not (isinstance(b, int) and bv == 0):
                        sp.wait_ge(vnlo_done, bv)
                    sp.dma_start(vn_raw[:, :], v_new[bass.ds(DEC_T * bv, DEC_T), :]).then_inc(vn_in, 16)
                if has(b, -1):
                    load_k(b + 1, 1 - u, None if isinstance(b, int) and b == 0 else 16 * b)
                if has(b, 1):
                    load_v(2, 8)
            all_turns(sp, body)
            sp.wait_ge(mgn_done, 1)
            sp.dma_start(c.merged_dram[:, :, SEQ:NTOK].rearrange("h p n -> p h n"), mg[:, :, :]).then_inc(mgn_out, 16)
            sp.wait_ge(mgn_out, 16)

        @block.tensor
        def _(pe):
            def body(b, u):
                for h in range(H + 1):
                    if h < H and has(b, 0):
                        if h == 0:
                            pe.wait_ge(k_in[u], 16 * NPAGES // 2 * (b - u) + 16 * NPAGES)
                        for hf in range(2):
                            if not (isinstance(b, int) and b == 0 and h == 0):
                                pe.wait_ge(ktlo_done, 16 * b + 2 * h + hf - 1)
                            for n in range(4):
                                last = pe.transpose(tb[hf][:, 128 * n:128 * (n + 1)],
                                                    k_raw[:, u, 4 * hf + n, 128 * h:128 * (h + 1)], c.ident[:, :])
                            last.then_inc(tk_done, 1)
                    if h >= 1 and has(b, 0):
                        g = h - 1
                        if g == 0:
                            if not (isinstance(b, int) and b == 0):
                                pe.wait_ge(ttr_done, b)
                            pe.wait_ge(qdlo_done, 2 * b + 2)
                        pe.wait_ge(ktlo_done, 16 * b + 2 * g + 2)
                        pe.wait_ge(ktn_lo, 8 * b + g + 1)
                        for cc in range(3):
                            keys = slice(SC * cc, SC * (cc + 1))
                            for x, (q, k) in enumerate(((qd_hi, kt_hi), (qd_hi, kt_lo), (qd_lo, kt_hi))):
                                last = pe.matmul(S3[:, cc, :], q[:, 128 * g:128 * (g + 1)], k[:, g % 2, keys],
                                                 start=(g == 0 and x == 0), stop=(g == H - 1 and x == 2))
                        last.then_inc(qkh_done, 1)
                    if h == 3 and has(b, 2):
                        pe.wait_ge(o2_done, b - 1)
                        pe.wait_ge(ptlo_done, 2 * (b - 1))
                        pe.sem_inc(pe_settled, 1)
                        for g in range(H):
                            last = pe.transpose(pt[:, NS * g:NS * (g + 1)], o2s[:, 128 * g:128 * (g + 1)],
                                                c.ident[0:NS, 0:NS])
                        last.then_inc(ot_done, 1)
                    if h == 5 and has(b, 1):
                        pe.wait_ge(c_done, b)
                        if has(b, 2):
                            pe.wait_ge(ots_done, b - 1)
                            pe.wait_ge(o2_done, b - 1)
                        for n in range(NPAGES):
                            pe.matmul(pt[:, NS * n:NS * (n + 1)], P[:, 128 * n:128 * (n + 1)], C[:, :],
                                      start=True, stop=True)
                        pe.matmul(ptn, P[:, PAST:NKEYS], C[:, :], start=True, stop=True,
                                  skip_group_check=True).then_inc(pt_done, 1)
                if has(b, 1):
                    pe.wait_ge(ptlo_done, 2 * b)
                    pe.wait_ge(vlo_done, 8 * b)
                    pe.wait_ge(vnlo_done, b)
                    if has(b, 2):
                        pe.wait_ge(o2_done, b - 1)
                    for hf in range(2):
                        cols = slice(512 * hf, 512 * (hf + 1))
                        for n in range(NPAGES + 1):
                            k = 128 if n < NPAGES else DEC_T
                            vh, vl = (v_hi[:, n, cols], v_lo[:, n, cols]) if n < NPAGES else (vn_hi[:, cols], vn_lo[:, cols])
                            for x, (w, v) in enumerate(((pt_hi, vh), (pt_hi, vl), (pt_lo, vh))):
                                last = pe.matmul(o2[:, cols], w[0:k, n, :], v,
                                                 start=(n == 0 and x == 0), stop=(n == NPAGES and x == 2))
                    last.then_inc(pv_done, 1)
            all_turns(pe, body)
            pe.wait_ge(sq_done, 1)
            pe.matmul(ps[:, 0, 0:H * NS], c.ones[:, :], P[:, 0:H * NS], start=True, stop=True).then_inc(ss_done, 1)

        @block.scalar
        def _(act):
            act.wait_ge(s_fill, 4)

            def queries(b):
                for m in range(2):
                    part = slice(64 * m, 64 * m + 64)
                    act.activation(qd_hi[part, :].rearrange("p (h x) -> p h x", h=H)[:, :, 8 * m:8 * m + 8],
                                   c.q_new[part, :, bass.ds(DEC_T * b, DEC_T)], ACT.Copy).then_inc(qdhi_done, 1)

            queries(0)

            def body(b, u):
                for h in range(H):
                    if has(b, 0):
                        for hf in range(2):
                            act.wait_ge(tk_done, 16 * b + 2 * h + hf + 1)
                            if hf == 0 and not (isinstance(b, int) and b == 0 and h < 2):
                                act.wait_ge(qkh_done, 8 * b + h - 1)
                            act.activation(kt_hi[:, h % 2, 512 * hf:512 * (hf + 1)], tb[hf], ACT.Copy)\
                               .then_inc(kthi_done, 1)
                        act.activation(kt_hi[:, h % 2, PAST:NKEYS], c.k_new[:, h, bass.ds(DEC_T * b, DEC_T)],
                                       ACT.Copy).then_inc(ktn_hi, 1)
                    if has(b, 1):
                        act.wait_ge(v_in[h % 2], 64 * b - 64 + 16 * (h // 2 + 1))
                        if h == 0 and has(b, 2):
                            act.wait_ge(pv_done, b - 1)
                        act.activation(v_hi[:, h, :], v_raw[:, h % 2, :], ACT.Copy).then_inc(vhi_done, 1)
                        if h == 0:
                            act.wait_ge(vn_in, 16 * b)
                            act.activation(vn_hi[:, :], vn_raw[:, :], ACT.Copy).then_inc(vnhi_done, 1)
                    if h == 3 and has(b, 2):
                        act.wait_ge(ot_done, b - 1)
                        diag = bass.AP(tensor=pt.tensor, offset=pt.offset, ap=[list(pt.ap[0]), [NS + DEC_T, H], [1, DEC_T]])
                        act.activation(oT[:, :, bass.ds(DEC_T * (b - 2), DEC_T)], diag, ACT.Copy).then_inc(ots_done, 1)
                    if h == 5 and has(b, 1):
                        act.wait_ge(pt_done, b)
                        act.activation(pt_hi[:, 0:NPAGES, :], pt.rearrange("p (n k) -> p n k", n=NPAGES), ACT.Copy)\
                           .then_inc(pthi_done, 1)
                        act.activation(pt_hi[0:DEC_T, NPAGES, :], ptn, ACT.Copy).then_inc(pthi_done, 1)
                if has(b, 0):
                    act.wait_ge(nmx_done, b + 1)
                    act.activation(P[:, :], P[:, :], ACT.Exp, bias=mx[:, 1:2], accum_out=mx[:, 2:3])\
                       .then_inc(exp_done, 1)
                    if has(b, -1):
                        queries(b + 1)
                if has(b, 1):
                    act.wait_ge(pv_done, b)
                    if has(b, 2):
                        act.wait_ge(ot_done, b - 1)
                    act.activation(o2s[:, :], o2, ACT.Copy).then_inc(o2_done, 1)
            all_turns(act, body)
            act.wait_ge(ots_done, DEC_B)
            act.activation(P[:, 0:H * NS], oT[:, :, :].rearrange("p h n -> p (h n)"), ACT.Square).then_inc(sq_done, 1)
            act.wait_ge(ss_done, 1)
            act.activation(P[:, 512:1024], ps[:, 0, 0:512], ACT.Ln, bias=eps[:, :], scale=1.0 / KV).then_inc(achain, 1)
            act.wait_ge(achain, 1)
            act.activation(P[:, 512:1024], P[:, 512:1024], ACT.Exp, scale=-0.5).then_inc(rst_done, 1)

        @block.vector
        def _(dve):
            n_ = [0]

            def link(ins_):
                n_[0] += 1
                ins_.then_inc(chain, 1)
                dve.wait_ge(chain, n_[0])

            dve.memset(qd_hi[:, :].bitcast(F32), 0.0).then_inc(s_fill, 1)
            dve.memset(qd_lo[:, :].bitcast(F32), 0.0).then_inc(s_fill, 1)
            dve.memset(eps[:, :], EPS).then_inc(s_fill, 1)
            dve.wait_ge(const_in, 32)
            link(dve.tensor_scalar(sgn[:, 0:1], c.neglam[:, :], -1.0, None, ALU.add))
            link(dve.tensor_tensor(sgn[:, 1:2], sgn[:, 0:1], sel[:, NS:NS + 1], ALU.mult))
            link(dve.tensor_scalar(sgn[:, 1:2], sgn[:, 1:2], 1.0, None, ALU.add))
            dve.sem_inc(s_fill, 1)

            def queries(b):
                for m in range(2):
                    part = slice(64 * m, 64 * m + 64)
                    view = (slice(None), slice(None), slice(8 * m, 8 * m + 8))
                    dve.wait_ge(qdhi_done, 2 * b + m + 1)
                    dve.tensor_tensor(qd_lo[part, :].rearrange("p (h x) -> p h x", h=H)[view],
                                      c.q_new[part, :, bass.ds(DEC_T * b, DEC_T)],
                                      qd_hi[part, :].bitcast(F32).rearrange("p (h x) -> p h x", h=H)[view],
                                      ALU.subtract).then_inc(qdlo_done, 1)

            queries(0)

            def body(b, u):
                for h in range(H):
                    if has(b, 0):
                        for hf in range(2):
                            dve.wait_ge(kthi_done, 16 * b + 2 * h + hf + 1)
                            keys = slice(512 * hf, 512 * (hf + 1))
                            dve.tensor_tensor(kt_lo[:, h % 2, keys], tb[hf], kt_hi[:, h % 2, keys].bitcast(F32),
                                              ALU.subtract).then_inc(ktlo_done, 1)
                        dve.wait_ge(ktn_hi, 8 * b + h + 1)
                        dve.tensor_tensor(kt_lo[:, h % 2, PAST:NKEYS], c.k_new[:, h, bass.ds(DEC_T * b, DEC_T)],
                                          kt_hi[:, h % 2, PAST:NKEYS].bitcast(F32), ALU.subtract).then_inc(ktn_lo, 1)
                    if has(b, 1):
                        dve.wait_ge(vhi_done, 8 * b - 8 + h + 1)
                        dve.tensor_tensor(v_lo[:, h, :], v_raw[:, h % 2, :], v_hi[:, h, :].bitcast(F32),
                                          ALU.subtract).then_inc(vlo_done, 1)
                        if h == 0:
                            dve.wait_ge(vnhi_done, b)
                            dve.tensor_tensor(vn_lo[:, :], vn_raw[:, :], vn_hi[:, :].bitcast(F32),
                                              ALU.subtract).then_inc(vnlo_done, 1)
                    if h == 5 and has(b, 1):
                        dve.wait_ge(pthi_done, 2 * b)
                        dve.tensor_tensor(pt_lo[:, 0:NPAGES, :], pt.rearrange("p (n k) -> p n k", n=NPAGES),
                                          pt_hi[:, 0:NPAGES, :].bitcast(F32), ALU.subtract).then_inc(ptlo_done, 1)
                        dve.tensor_tensor(pt_lo[0:DEC_T, NPAGES, :], ptn, pt_hi[0:DEC_T, NPAGES, :].bitcast(F32),
                                          ALU.subtract).then_inc(ptlo_done, 1)
                if has(b, 0):
                    dve.wait_ge(qkh_done, 8 * b + 8)
                    if has(b, 1):
                        dve.wait_ge(pt_done, b)
                        dve.sem_inc(dve_settled, 1)
                    dve.tensor_tensor_reduce(out=P[:, :].rearrange("p (a n) -> p a n", a=3), in0=S3,
                                             in1=sbias[:, :].rearrange("p (a n) -> p a n", a=3), scale=1.0,
                                             scalar=-3e38, op0=ALU.add, op1=ALU.max,
                                             accum_out=mx[:, 0:1]).then_inc(ttr_done, 1)
                    dve.wait_ge(ttr_done, b + 1)
                    dve.tensor_scalar(mx[:, 1:2], mx[:, 0:1], -1.0, None, ALU.mult).then_inc(nmx_done, 1)
                    dve.wait_ge(exp_done, b + 1)
                    dve.reciprocal(mx[:, 3:4], mx[:, 2:3]).then_inc(chain, 1)
                    dve.wait_ge(chain, 3 + 2 * b + 1)
                    dve.tensor_tensor(mx[:, 3:4], mx[:, 3:4], sgn[:, 1:2], ALU.mult).then_inc(chain, 1)
                    dve.wait_ge(chain, 3 + 2 * b + 2)
                    dve.tensor_scalar(C[:, :], sel[:, 0:NS], mx[:, 3:4], None, ALU.mult).then_inc(c_done, 1)
                    if has(b, -1):
                        queries(b + 1)
            all_turns(dve, body)
            dve.wait_ge(rst_done, 1)
            dve.wait_ge(ga_in, 16)
            n_[0] = 3 + 2 * DEC_B
            rst = P[:, 512:1024]
            of = oT[:, :, :].rearrange("p h n -> p (h n)")
            mf = mg[:, :, :].rearrange("p h n -> p (h n)")
            link(dve.scalar_tensor_tensor(out=of, in0=of, scalar=c.gsub[:, :], in1=rst, op0=ALU.mult, op1=ALU.mult))
            link(dve.tensor_tensor(of, of, c.gb_new[:, :, :].rearrange("p h n -> p (h n)"), ALU.mult))
            dve.tensor_tensor(mf, mf, of, ALU.add).then_inc(mgn_done, 1)


def out_projection(nc, sb, sem, ins, c):
    ps = c.ps
    raw = sb("o_raw", [128, 2, KT, 128], F32)
    w_hi = sb("o_w_hi", [128, KT, D], F32R)
    w_lo = sb("o_w_lo", [128, KT, D], F32R)
    m_hi = sb("m_hi", [128, 2, KT, 128], F32R)
    m_lo = sb("m_lo", [128, 2, KT, 128], F32R)
    xn = sb("o_xn", [128, 2, D], F32)
    g = sb("o_g", [128, D], F32)
    st = sb("o_st", [128, 2, 3], F32)
    eps = sb("o_eps", [128, 1], F32)
    raw_in = [sem("o_raw_in0"), sem("o_raw_in1")]
    x_in = [sem("o_x_in0"), sem("o_x_in1")]
    g_in = sem("o_g_in")
    eps_set = sem("o_eps_set")
    hi_done = sem("o_hi_done")
    lo_done = sem("o_lo_done")
    mm_done = sem("o_mm_done")
    x2_done = sem("x2_done")
    ssq_done = sem("o_ssq_done")
    std_done = sem("o_std_done")
    inv_done = sem("o_inv_done")
    xn_done = sem("o_xn_done")
    t_done = sem("o_t_done")
    h2hi_done = sem("h2hi_done")
    h2lo_done = sem("h2lo_done")
    merged = c.merged_dram.rearrange("k p n -> p k n")
    xp, xs = flat(ins["x_prompt"]), flat(ins["x_sample"])

    def all_turns(eng, body):
        body(0, 0)
        with eng.Fori(0, 3) as i:
            body(2 * i + 1, 1)
            body(2 * i + 2, 0)
        for t in range(7, 10):
            body(t, t % 2)

    def nrow(t):
        return NS if isinstance(t, int) and t == 8 else 128

    with nc.Block() as block:
        @block.sync
        def _(sp):
            sp.dma_start(g[:, :], broadcast_row(ins["norm_ffn"], 128)).then_inc(g_in, 16)
            w_out = ins["w_out"].rearrange("o (k p) n -> p (o k) n", p=128)
            for k in range(KT):
                if k >= 2:
                    sp.wait_ge(lo_done, k - 1)
                sp.dma_start(raw[:, k % 2, :, :].rearrange("p k n -> p (k n)"), w_out[:, k, :])\
                  .then_inc(raw_in[k % 2], 16)

            def body(t, u):
                if isinstance(t, int) and t > 8:
                    return
                n = nrow(t)
                sp.wait_ge(lo_done, KT + t - 1)
                sp.dma_start(raw[:, u, :, 0:n], merged[:, :, bass.ds(128 * t, n)]).then_inc(raw_in[u], 16)
                src = xs[:, :] if n == NS else xp[bass.ds(128 * t, 128), :]
                sp.dma_start(c.x2[0:n, bass.ds(t, 1), :].rearrange("p a n -> p (a n)"), src).then_inc(x_in[u], 16)
            all_turns(sp, body)

        @block.scalar
        def _(act):
            act.wait_ge(eps_set, 1)
            for k in range(KT):
                act.wait_ge(raw_in[k % 2], 16 * (k // 2 + 1))
                act.activation(w_hi[:, k, :], raw[:, k % 2, :, :].rearrange("p k n -> p (k n)"), ACT.Copy)\
                   .then_inc(hi_done, 1)

            def split(t, u):
                n = nrow(t)
                act.wait_ge(raw_in[u], 8 * (t - u) + 64 + 16)
                act.wait_ge(mm_done, t + 1)
                act.activation(m_hi[:, u, :, 0:n], raw[:, u, :, 0:n], ACT.Copy).then_inc(hi_done, 1)

            split(0, 0)

            def body(t, u):
                if not (isinstance(t, int) and t > 7):
                    split(t + 1, 1 - u)
                if not (isinstance(t, int) and t == 0):
                    s, v = t - 1, 1 - u
                    for q in range(2):
                        n = NS if isinstance(t, int) and t == 9 else 128
                        act.wait_ge(t_done, 2 * s + q + 5)
                        act.activation(c.h2_hi[:, 4 * q:4 * q + 4, bass.ds(128 * s, n)],
                                       ps[:, 4 + 2 * v + q, :].rearrange("p (k n) -> p k n", k=4)[:, :, 0:n],
                                       ACT.Copy).then_inc(h2hi_done, 1)
                if not (isinstance(t, int) and t > 8):
                    n = nrow(t)
                    act.wait_ge(x2_done, t + 3)
                    act.wait_ge(t_done, 2 * t + 2)
                    act.activation(xn[0:n, u, :], c.x2[0:n, bass.ds(t, 1), :].rearrange("p a n -> p (a n)"),
                                   ACT.Square, accum_out=st[0:n, u, 0:1]).then_inc(ssq_done, 1)
                    act.wait_ge(ssq_done, t + 1)
                    act.activation(st[0:n, u, 1:2], st[0:n, u, 0:1], ACT.Sqrt, bias=eps[0:n, :],
                                   scale=1.0 / D).then_inc(std_done, 1)
            all_turns(act, body)

        @block.vector
        def _(dve):
            dve.memset(eps[:, :], EPS).then_inc(eps_set, 1)
            dve.sem_inc(x2_done, 2)
            dve.sem_inc(h2lo_done, 4)
            for k in range(KT):
                dve.wait_ge(hi_done, k + 1)
                dve.tensor_tensor(w_lo[:, k, :], raw[:, k % 2, :, :].rearrange("p k n -> p (k n)"),
                                  w_hi[:, k, :].bitcast(F32), ALU.subtract).then_inc(lo_done, 1)
            dve.wait_ge(g_in, 16)

            def split(t, u):
                n = nrow(t)
                dve.wait_ge(hi_done, KT + t + 1)
                dve.tensor_tensor(m_lo[:, u, :, 0:n], raw[:, u, :, 0:n], m_hi[:, u, :, 0:n].bitcast(F32),
                                  ALU.subtract).then_inc(lo_done, 1)

            split(0, 0)

            def body(t, u):
                if not (isinstance(t, int) and t > 7):
                    split(t + 1, 1 - u)
                if not (isinstance(t, int) and t == 0):
                    s, v = t - 1, 1 - u
                    n = NS if isinstance(t, int) and t == 9 else 128
                    cols = bass.ds(128 * s, n)
                    for q in range(2):
                        dve.wait_ge(h2hi_done, 2 * s + q + 1)
                        dve.tensor_tensor(c.h2_lo[:, 4 * q:4 * q + 4, cols],
                                          ps[:, 4 + 2 * v + q, :].rearrange("p (k n) -> p k n", k=4)[:, :, 0:n],
                                          c.h2_hi[:, 4 * q:4 * q + 4, cols].bitcast(F32), ALU.subtract)\
                           .then_inc(h2lo_done, 1)
                if not (isinstance(t, int) and t > 8):
                    n = nrow(t)
                    x2 = c.x2[0:n, bass.ds(t, 1), :].rearrange("p a n -> p (a n)")
                    dve.wait_ge(x_in[u], 8 * (t - u) + 16)
                    dve.wait_ge(mm_done, t + 3)
                    dve.tensor_tensor(x2, x2, ps[0:n, 2 * u:2 * u + 2, :].rearrange("p a n -> p (a n)"),
                                      ALU.add).then_inc(x2_done, 1)
                    dve.wait_ge(std_done, t + 1)
                    dve.reciprocal(st[0:n, u, 2:3], st[0:n, u, 1:2]).then_inc(inv_done, 1)
                    dve.wait_ge(inv_done, t + 1)
                    dve.scalar_tensor_tensor(out=xn[0:n, u, :], in0=x2, scalar=st[0:n, u, 2:3], in1=g[0:n, :],
                                             op0=ALU.mult, op1=ALU.mult).then_inc(xn_done, 1)
            all_turns(dve, body)

        @block.tensor
        def _(pe):
            pe.sem_inc(mm_done, 2)
            pe.sem_inc(t_done, 4)

            def body(t, u):
                if not (isinstance(t, int) and t > 8):
                    n = nrow(t)
                    pe.wait_ge(lo_done, KT + t + 1)
                    pe.wait_ge(x2_done, t + 1)
                    for hf in range(2):
                        cols = slice(512 * hf, 512 * (hf + 1))
                        for k in range(KT):
                            for i, (m, w) in enumerate(((m_hi, w_hi), (m_hi, w_lo), (m_lo, w_hi))):
                                last = pe.matmul(ps[0:n, 2 * u + hf, :], m[:, u, k, 0:n], w[:, k, cols],
                                                 start=(k == 0 and i == 0), stop=(k == KT - 1 and i == 2))
                    last.then_inc(mm_done, 1)
                if not (isinstance(t, int) and t == 0):
                    s, v = t - 1, 1 - u
                    n = NS if isinstance(t, int) and t == 9 else 128
                    pe.wait_ge(xn_done, s + 1)
                    pe.wait_ge(h2lo_done, 2 * s + 2)
                    for q in range(2):
                        for k in range(4):
                            last = pe.transpose(ps[:, 4 + 2 * v + q, 128 * k:128 * k + n],
                                                xn[0:n, v, 512 * q + 128 * k:512 * q + 128 * (k + 1)],
                                                c.ident[0:n, 0:n])
                        last.then_inc(t_done, 1)
            all_turns(pe, body)


GF = 3
NG = DFF // 128 // GF
NT = 9
NUP = 6 * GF


def mixer(nc, sb, sem, ins, outs, c):
    ps = c.ps
    raw = sb("f_raw", [128, 3, KT, 128], F32)
    w_hi = sb("f_w_hi", [128, 2, KT, 128], F32R)
    w_lo = sb("f_w_lo", [128, 2, KT, 128], F32R)
    d_hi = sb("d_hi", [128, GF, D], F32R)
    d_lo = sb("d_lo", [128, GF, D], F32R)
    a_hi = sb("a_hi", [128, GF, NTOK], F32R)
    a_lo = sb("a_lo", [128, GF, NTOK], F32R)
    gl = sb("gl", [128, NTOK], F32)
    yc = sb("yc", [128, 3, 384], F32)
    carry = sb("f_carry", [128, 2, 2], F32)
    fprm = sb("fprm", [128, 2, DFF // 128, FROW], F32)
    NST = (FCONV_W - 1) * (1 + DEC_B)
    stc = sb("f_stc", [128, 2 * GF, NST], F32)
    st_rows = sb("f_st_rows", [NST, 2, 128 * GF], F32)
    prm = sb("f_prm", [128, 2, FROW], F32)
    raw_in = [sem(f"f_raw_in{u}") for u in range(3)]
    prm_in = sem("f_prm_in")
    prm_done = sem("f_prm_done")
    whi_done = sem("f_whi_done")
    wlo_done = sem("f_wlo_done")
    dhi_done = sem("dhi_done")
    dlo_done = sem("dlo_done")
    up_done = sem("up_done")
    y_done = sem("f_y_done")
    cv_done = sem("cv_done")
    gl_done = sem("gl_done")
    av_done = sem("av_done")
    ahi_done = sem("ahi_done")
    alo_done = sem("alo_done")
    stc_done = sem("f_stc_done")
    st_t = sem("f_st_t")
    pe_settled = sem("f_pe_settled")
    sp_settled = sem("f_sp_settled")
    str_done = sem("f_str_done")
    st_out = sem("f_st_out")
    dn_done = sem("dn_done")
    add_done = sem("add_done")
    chain = sem("f_chain")
    LINKS = c.mixer_links
    w_up = ins["w_up"].rearrange("o (k p) n -> p (o k) n", p=128)
    w_dn = ins["w_down"].rearrange("o (k p) n -> p (o k) n", p=128)

    turn = []
    for j in range(GF):
        for p in range(2):
            for cc in range(3):
                if cc == 0:
                    turn.append(("W", 2 * j + p + 1))
                turn.append(("U", j, p, cc))
                if j == 0 and p == 0 and cc == 1:
                    turn.append(("DN",))
                if j > 0 and p == 0 and cc == 1:
                    turn.append(("DW", j - 1))
                if j == GF - 1 and p == 1 and cc == 1:
                    turn.append(("DW", GF - 1))
    raws = [s for s in turn if s[0] in ("W", "DW")]
    NRAW = len(raws)

    def all_turns(eng, body):
        body(0)
        with eng.Fori(1, NG - 1) as f:
            body(f)
        body(NG - 1)

    def first(f):
        return isinstance(f, int) and f == 0

    def last_(f):
        return isinstance(f, int) and f == NG - 1

    def wait_before(eng, semaphore, f, per, i, back):
        if not (first(f) and i - back < 0):
            eng.wait_ge(semaphore, per * f + i - back + 1)

    with nc.Block() as block:
        @block.sync
        def _(sp):
            sp.dma_start(fprm[:, :, :, :], c.fprm_dram.rearrange("p (a k r) -> p a k r", a=2, r=FROW))\
              .then_inc(prm_in, 16)

            def load(f, r):
                kind, i = raws[r % NRAW]
                f = f + r // NRAW
                if kind == "W":
                    f = f + i // (2 * GF)
                    i = i % (2 * GF)
                    col = 128 * GF * f + (128 * (i // 2) + DFF * (i % 2))
                    sp.dma_start(raw[:, (r + 1) % 3, :, :], w_up[:, :, bass.ds(col, 128)])\
                      .then_inc(raw_in[(r + 1) % 3], 16)
                else:
                    sp.dma_start(raw[:, (r + 1) % 3, :, :].rearrange("p k n -> p (k n)"),
                                 w_dn[:, bass.ds(GF * f + i, 1), :].rearrange("p a n -> p (a n)"))\
                      .then_inc(raw_in[(r + 1) % 3], 16)

            sp.dma_start(raw[:, 0, :, :], w_up[:, :, 0:128]).then_inc(raw_in[0], 16)
            load(0, 0)
            load(0, 1)

            def store_states(f):
                sp.wait_ge(str_done, f + 1)
                sp.sem_inc(sp_settled, 1)
                for p in range(2):
                    col = 128 * GF * f + DFF * p
                    sp.dma_start(flat(outs["ffn_conv_prompt"])[:, bass.ds(col, 128 * GF)],
                                 st_rows[0:2, p, :]).then_inc(st_out, 16)
                    sp.dma_start(flat(outs["ffn_conv_sample"])[:, bass.ds(col, 128 * GF)],
                                 st_rows[2:NST, p, :]).then_inc(st_out, 16)

            def body(f):
                r = 0
                for s in turn:
                    if s[0] in ("W", "DW"):
                        if not (last_(f) and (r + 2 >= NRAW or raws[r + 2] == ("W", 2 * GF))):
                            kind, i = raws[r - 1] if r > 0 else ("W", 0) if first(f) else ("DW", -1)
                            if kind == "W":
                                sp.wait_ge(wlo_done, 2 * GF * f + i + 1)
                            else:
                                sp.wait_ge(dlo_done, GF * f + i + 1)
                            load(f, r + 2)
                        r += 1
                    if s[0] == "DN" and not first(f):
                        store_states(f - 1)
            all_turns(sp, body)
            store_states(NG - 1)
            sp.wait_ge(st_out, 64 * NG)

        def raw_wait(eng, f, r):
            eng.wait_ge(raw_in[(r + 1) % 3], 16 * (NRAW // 3) * f + 16 * ((r + 1) // 3) + 16)

        @block.tensor
        def _(pe):
            def down(f):
                pe.wait_ge(alo_done, 3 * GF * (f + 1))
                pe.wait_ge(dlo_done, GF * (f + 1))
                for t in range(NT):
                    n = NS if t == NT - 1 else 128
                    for hf in range(2):
                        e = 2 * t + hf
                        pe.wait_ge(add_done, 2 * NT * f + e + 1)
                        if e == 0 and not first(f):
                            pe.wait_ge(str_done, f)
                        for j in range(GF):
                            for i, (a, w) in enumerate(((a_hi, d_hi), (a_hi, d_lo), (a_lo, d_hi))):
                                l_ = pe.matmul(ps[0:n, 6 + e % 2, :], a[:, j, 128 * t:128 * t + n],
                                               w[:, j, 512 * hf:512 * (hf + 1)],
                                               start=(j == 0 and i == 0), stop=(j == GF - 1 and i == 2))
                        l_.then_inc(dn_done, 1)
                pe.wait_ge(stc_done, 2 * GF * (f + 1))
                pe.wait_ge(add_done, 2 * NT * (f + 1) + 2)
                pe.sem_inc(pe_settled, 1)
                for i in range(2 * GF):
                    l_ = pe.transpose(ps[0:NST, 6 + i % 2, 128 * (i // 2):128 * (i // 2 + 1)], stc[:, i, :],
                                      c.ident[:, :])
                l_.then_inc(st_t, 1)

            def body(f):
                e = 0
                for s in turn:
                    if s[0] == "U":
                        j, p, cc = s[1:]
                        off, n = CHUNKS[cc]
                        if cc == 0:
                            pe.wait_ge(wlo_done, 2 * GF * f + 2 * j + p + 1)
                        wait_before(pe, cv_done, f, NUP, e, 6)
                        for k in range(KT):
                            for i, (w, x) in enumerate(((w_hi, c.h2_hi), (w_hi, c.h2_lo), (w_lo, c.h2_hi))):
                                l_ = pe.matmul(ps[:, e % 6, 0:n], w[:, p, k, :], x[:, k, off:off + n],
                                               start=(k == 0 and i == 0), stop=(k == KT - 1 and i == 2))
                        l_.then_inc(up_done, 1)
                        e += 1
                    elif s[0] == "DN" and not first(f):
                        down(f - 1)
            all_turns(pe, body)
            down(NG - 1)

        @block.scalar
        def _(act):
            act.wait_ge(prm_in, 16)

            def split_up(f, i, r):
                raw_wait(act, f, r)
                if not (first(f) and i < 2):
                    act.wait_ge(up_done, NUP * f + 3 * (i - 1))
                act.activation(w_hi[:, i % 2, :, :], raw[:, (r + 1) % 3, :, :], ACT.Copy).then_inc(whi_done, 1)

            split_up(0, 0, -1)

            def state_rows(f):
                act.wait_ge(st_t, f + 1)
                if not first(f):
                    act.wait_ge(st_out, 64 * f)
                act.activation(st_rows[:, :, :], ps[0:NST, 6:8, 0:128 * GF], ACT.Copy).then_inc(str_done, 1)

            def finish(f, e):
                j, p, cc = e // 6, e // 3 % 2, e % 3
                off, n = CHUNKS[cc]
                if p == 0:
                    act.wait_ge(cv_done, NUP * f + e + 1)
                    wait_before(act, av_done, f, 3 * GF, 3 * j + cc, 3)
                    act.activation(gl[:, off:off + n], yc[:, e % 3, 0:n], ACT.Gelu_apprx_tanh)\
                       .then_inc(gl_done, 1)
                else:
                    act.wait_ge(av_done, 3 * GF * f + 3 * j + cc + 1)
                    if j == 0 and cc == 0 and not first(f):
                        act.wait_ge(dn_done, 2 * NT * f)
                    act.activation(a_hi[:, j, off:off + n], yc[:, e % 3, 0:n], ACT.Copy)\
                       .then_inc(ahi_done, 1)

            def body(f):
                e = r = 0
                for s in turn:
                    if s[0] == "W":
                        if not (s[1] == 2 * GF and last_(f)):
                            split_up(f, s[1], r)
                        r += 1
                    elif s[0] == "DN" and not first(f):
                        state_rows(f - 1)
                    elif s[0] == "DW":
                        j = s[1]
                        raw_wait(act, f, r)
                        if j == 0 and not first(f):
                            act.wait_ge(dn_done, 2 * NT * f)
                        act.activation(d_hi[:, j, :], raw[:, (r + 1) % 3, :, :].rearrange("p k n -> p (k n)"),
                                       ACT.Copy).then_inc(dhi_done, 1)
                        r += 1
                    elif s[0] == "U":
                        j, p, cc = s[1:]
                        off, n = CHUNKS[cc]
                        act.wait_ge(up_done, NUP * f + e + 1)
                        act.wait_ge(prm_done, 2 * GF * f + 2 * j + p + 1)
                        if p == 1:
                            act.wait_ge(gl_done, 3 * GF * f + 3 * j + cc + 1)
                        else:
                            wait_before(act, av_done, f, 3 * GF, 3 * j + cc, 3)
                            wait_before(act, ahi_done, f, 3 * GF, 3 * j + cc, 3)
                            wait_before(act, alo_done, f, 3 * GF, 3 * j + cc, 3)
                        act.activation(yc[:, e % 3, 0:n], ps[:, e % 6, 0:n], ACT.Identity,
                                       bias=prm[:, p, FCONV_W:FCONV_W + 1],
                                       scale=prm[:, p, FCONV_W - 1:FCONV_W]).then_inc(y_done, 1)
                        if e > 0:
                            finish(f, e - 1)
                        elif not first(f):
                            finish(f - 1, NUP - 1)
                        e += 1
            all_turns(act, body)
            finish(NG - 1, NUP - 1)
            state_rows(NG - 1)

        @block.vector
        def _(dve):
            dve.sem_inc(add_done, 2)
            dve.wait_ge(prm_in, 16)

            def add(f):
                for t in range(NT):
                    n = NS if t == NT - 1 else 128
                    for hf in range(2):
                        e = 2 * t + hf
                        x2 = c.x2[0:n, t, 512 * hf:512 * (hf + 1)]
                        dve.wait_ge(dn_done, 2 * NT * f + e + 1)
                        dve.tensor_tensor(x2, x2, ps[0:n, 6 + e % 2, :], ALU.add).then_inc(add_done, 1)

            def split_up(f, i, r):
                dve.wait_ge(whi_done, 2 * GF * f + i + 1)
                dve.tensor_tensor(w_lo[:, i % 2, :, :], raw[:, (r + 1) % 3, :, :], w_hi[:, i % 2, :, :].bitcast(F32),
                                  ALU.subtract).then_inc(wlo_done, 1)

            split_up(0, 0, -1)

            def low_part(f, e):
                j, p, cc = e // 6, e // 3 % 2, e % 3
                off, n = CHUNKS[cc]
                if p == 1:
                    dve.wait_ge(ahi_done, 3 * GF * f + 3 * j + cc + 1)
                    dve.tensor_tensor(a_lo[:, j, off:off + n], yc[:, e % 3, 0:n],
                                      a_hi[:, j, off:off + n].bitcast(F32), ALU.subtract).then_inc(alo_done, 1)

            def body(f):
                n_ = [0]

                def link(ins_):
                    n_[0] += 1
                    ins_.then_inc(chain, 1)
                    dve.wait_ge(chain, LINKS * f + n_[0])

                e = m = r = 0
                for s in turn:
                    if s[0] == "W":
                        if not (s[1] == 2 * GF and last_(f)):
                            split_up(f, s[1], r)
                        r += 1
                    elif s[0] == "DW":
                        j = s[1]
                        dve.wait_ge(dhi_done, GF * f + j + 1)
                        dve.tensor_tensor(d_lo[:, j, :], raw[:, (r + 1) % 3, :, :].rearrange("p k n -> p (k n)"),
                                          d_hi[:, j, :].bitcast(F32), ALU.subtract).then_inc(dlo_done, 1)
                        r += 1
                    elif s[0] == "DN" and not first(f):
                        add(f - 1)
                    elif s[0] == "U":
                        j, p, cc = s[1:]
                        off, n = CHUNKS[cc]
                        np_ = PROMPT_OF[cc]
                        x = ps[:, e % 6, :]
                        y = yc[:, e % 3, :]
                        w = [prm[:, p, k:k + 1] for k in range(FCONV_W)]
                        if cc == 0:
                            if not (first(f) and 2 * j + p < 2):
                                dve.wait_ge(y_done, NUP * f + 3 * (2 * j + p - 1))
                            dve.tensor_copy(prm[:, p, :], fprm[:, p, bass.ds(GF * f + j, 1), :]
                                            .rearrange("p a n -> p (a n)")).then_inc(prm_done, 1)
                            dve.wait_ge(prm_done, 2 * GF * f + 2 * j + p + 1)
                        dve.wait_ge(y_done, NUP * f + e + 1)
                        link(dve.scalar_tensor_tensor(out=y[:, 1:np_], in0=x[:, 0:np_ - 1], scalar=w[1],
                                                      in1=y[:, 1:np_], op0=ALU.mult, op1=ALU.add))
                        link(dve.scalar_tensor_tensor(out=y[:, 2:np_], in0=x[:, 0:np_ - 2], scalar=w[0],
                                                      in1=y[:, 2:np_], op0=ALU.mult, op1=ALU.add))
                        if cc > 0:
                            old = carry[:, (cc - 1) % 2, :]
                            link(dve.scalar_tensor_tensor(out=y[:, 0:2], in0=old, scalar=w[0], in1=y[:, 0:2],
                                                          op0=ALU.mult, op1=ALU.add))
                            link(dve.scalar_tensor_tensor(out=y[:, 0:1], in0=old[:, 1:2], scalar=w[1],
                                                          in1=y[:, 0:1], op0=ALU.mult, op1=ALU.add))
                        if cc < 2:
                            link(dve.tensor_copy(carry[:, cc % 2, :], x[:, np_ - 2:np_]))
                        else:
                            xs = x[:, np_:n].rearrange("p (b t) -> p b t", b=DEC_B)
                            ys = y[:, np_:n].rearrange("p (b t) -> p b t", b=DEC_B)
                            state = prm[:, p, FCONV_W + 1:FROW].rearrange("p (b t) -> p b t", b=DEC_B)
                            for out_, in_, k in ((ys[:, :, 1:], xs[:, :, 0:DEC_T - 1], 1),
                                                 (ys[:, :, 2:], xs[:, :, 0:DEC_T - 2], 0),
                                                 (ys[:, :, 0:2], state, 0), (ys[:, :, 0:1], state[:, :, 1:2], 1)):
                                link(dve.scalar_tensor_tensor(out=out_, in0=in_, scalar=w[k], in1=out_,
                                                              op0=ALU.mult, op1=ALU.add))
                            if m == 0 and not first(f):
                                dve.wait_ge(st_t, f)
                            link(dve.tensor_copy(stc[:, m, 0:2], x[:, np_ - 2:np_]))
                            dve.tensor_copy(stc[:, m, 2:NST].rearrange("p (b t) -> p b t", b=DEC_B),
                                            xs[:, :, DEC_T - 2:DEC_T]).then_inc(stc_done, 1)
                            dve.wait_ge(stc_done, 2 * GF * f + m + 1)
                            m += 1
                        dve.sem_inc(cv_done, 1)
                        if p == 1:
                            dve.wait_ge(gl_done, 3 * GF * f + 3 * j + cc + 1)
                            dve.tensor_tensor(y[:, 0:n], y[:, 0:n], gl[:, off:off + n], ALU.mult).then_inc(av_done, 1)
                        if e > 0:
                            low_part(f, e - 1)
                        elif not first(f):
                            low_part(f - 1, NUP - 1)
                        e += 1
                assert n_[0] == LINKS, ("MIXER_LINKS", n_[0])
            all_turns(dve, body)
            low_part(NG - 1, NUP - 1)
            add(NG - 1)


def final_norm(nc, sb, sem, ins, outs, c):
    y = sb("y", [128, 3, D], F32)
    junk = sb("y_junk", [128, D], F32)
    g = sb("y_g", [128, D], F32)
    st = sb("y_st", [128, NT, 3], F32)
    eps = sb("y_eps", [128, 1], F32)
    g_in = sem("y_g_in")
    eps_set = sem("y_eps_set")
    ssq_done = sem("y_ssq_done")
    std_done = sem("y_std_done")
    inv_done = sem("y_inv_done")
    y_done = sem("y_y_done")
    y_out = [sem(f"y_out{u}") for u in range(3)]
    yp, ys = flat(outs["y_prompt"]), flat(outs["y_sample"])

    with nc.Block() as block:
        @block.sync
        def _(sp):
            sp.dma_start(g[:, :], broadcast_row(ins["norm_final"], 128)).then_inc(g_in, 16)
            for t in range(NT):
                sp.wait_ge(y_done, t + 1)
                if t < NT - 1:
                    sp.dma_start(yp[128 * t:128 * (t + 1), :], y[:, t % 3, :]).then_inc(y_out[t % 3], 16)
                else:
                    sp.dma_start(ys[:, :], y[0:NS, t % 3, :]).then_inc(y_out[t % 3], 16)
            for u in range(3):
                sp.wait_ge(y_out[u], 48)

        @block.scalar
        def _(act):
            act.wait_ge(eps_set, 1)
            for t in range(NT):
                n = NS if t == NT - 1 else 128
                if t > 0:
                    act.wait_ge(std_done, t)
                act.activation(junk[0:n, :], c.x2[0:n, t, :], ACT.Square, accum_out=st[0:n, t, 0:1])\
                   .then_inc(ssq_done, 1)
                act.wait_ge(ssq_done, t + 1)
                act.activation(st[0:n, t, 1:2], st[0:n, t, 0:1], ACT.Sqrt, bias=eps[0:n, :], scale=1.0 / D)\
                   .then_inc(std_done, 1)

        @block.vector
        def _(dve):
            dve.memset(eps[:, :], EPS).then_inc(eps_set, 1)
            dve.wait_ge(g_in, 16)
            for t in range(NT):
                n = NS if t == NT - 1 else 128
                dve.wait_ge(std_done, t + 1)
                dve.reciprocal(st[0:n, t, 2:3], st[0:n, t, 1:2]).then_inc(inv_done, 1)
                dve.wait_ge(inv_done, t + 1)
                if t >= 3:
                    dve.wait_ge(y_out[t % 3], 16 * (t // 3))
                dve.scalar_tensor_tensor(out=y[0:n, t % 3, :], in0=c.x2[0:n, t, :], scalar=st[0:n, t, 2:3],
                                         in1=g[0:n, :], op0=ALU.mult, op1=ALU.mult).then_inc(y_done, 1)


INPUTS = ["x_prompt", "x_sample", "cache_k", "cache_v", "page_table", "state_rglru_h", "state_rglru_conv",
          "state_ffn_conv", "w_in", "conv_w", "conv_b", "rg_w_a", "rg_b_a", "rg_w_x", "rg_b_x", "rg_a_param",
          "lambda_q1", "lambda_k1", "lambda_q2", "lambda_k2", "subln_g", "rel_bias", "w_out", "norm_attn",
          "norm_ffn", "w_up", "ffn_conv_w", "ffn_conv_b", "w_down", "norm_final"]
OUTPUTS = [("y_prompt", (1, SEQ, D)), ("y_sample", (DEC_B, DEC_T, D)),
           ("k_rows_prompt", (1, 1, SEQ, H, KV)), ("v_rows_prompt", (1, 1, SEQ, H, KV)),
           ("k_rows_sample", (1, DEC_B, DEC_T, H, KV)), ("v_rows_sample", (1, DEC_B, DEC_T, H, KV)),
           ("rglru_h_prompt", (1, 1, D)), ("rglru_h_sample", (1, DEC_B, D)),
           ("rglru_conv_prompt", (1, 1, CONV_W - 1, D)), ("rglru_conv_sample", (1, DEC_B, CONV_W - 1, D)),
           ("ffn_conv_prompt", (1, 1, FCONV_W - 1, 2 * DFF)),
           ("ffn_conv_sample", (1, DEC_B, FCONV_W - 1, 2 * DFF))]


class Shared:
    pass


def build(nc, ins, outs):
    c = Shared()
    c.bias_rows_dram = nc.dram_tensor("bias_rows_dram", (H, NU), F32, kind="Internal").ap()
    c.bias_tiles_dram = nc.dram_tensor("bias_tiles_dram", (H, 128, BW), F32, kind="Internal").ap()
    c.fprm_dram = nc.dram_tensor("fprm_dram", (128, 2 * DFF // 128 * FROW), F32, kind="Internal").ap()
    c.sbias_dram = nc.dram_tensor("sbias_dram", (1, 128, NKEYS), F32, kind="Internal").ap()
    c.merged_dram = nc.dram_tensor("merged_dram", (H, 128, NTOK), F32, kind="Internal").ap()
    with ExitStack() as whole:
        def scope(stack):
            return lambda name, shape, dt: stack.enter_context(nc.sbuf_tensor(name, shape, dt))

        @contextmanager
        def semaphores():
            with ExitStack() as stack:
                mine = []

                def sem(name):
                    mine.append(stack.enter_context(nc.semaphore(name)))
                    return mine[-1]
                yield sem
                with nc.Block() as block:
                    @block.gpsimd
                    def _(pool):
                        for s in mine:
                            pool.sem_clear(s)

        sb = scope(whole)
        c.ps = whole.enter_context(nc.psum_tensor("ps", [128, 8, 512], F32))
        c.ident = sb("ident", [128, 128], F32)
        c.ones = sb("ones", [128, 128], F32)
        c.prm = sb("prm", [128, KT, NROW + 1], F32)
        c.gsub = sb("gsub", [128, 1], F32)
        c.neglam = sb("neglam", [128, 1], F32)
        c.mixer_links = MIXER_LINKS
        c.links = (DVE_LINKS_HEADS, ACT_LINKS_HEADS)
        with ExitStack() as part, semaphores() as sem:
            setup(nc, scope(part), sem, ins, c)
        upto_merge = ExitStack()
        c.q_new = scope(upto_merge)("q_new", [128, H, NS], F32)
        c.k_new = scope(upto_merge)("k_new", [128, H, NS], F32)
        c.gb_new = scope(upto_merge)("gb_new", [128, H, NS], F32)
        with ExitStack() as part:
            c.h_hi = scope(part)("h_hi", [128, KT, NTOK], F32R)
            c.h_lo = scope(part)("h_lo", [128, KT, NTOK], F32R)
            xp = flat(ins["x_prompt"])
            xsm = flat(ins["x_sample"])

            def load(eng, t, dst):
                if isinstance(t, int):
                    return eng.dma_start(dst, xsm[:, :])
                return eng.dma_start(dst, xp[bass.ds(128 * t, 128), :])
            with ExitStack() as inner, semaphores() as sem:
                norm_tiles(nc, scope(inner), sem, "n1", load, ins["norm_attn"], c.h_hi, c.h_lo, c.ident, c.ps)
            with ExitStack() as inner, semaphores() as sem:
                heads(nc, scope(inner), sem, ins, outs, c)
        with ExitStack() as part, semaphores() as sem:
            sampled(nc, scope(part), sem, ins, outs, c)
        upto_merge.close()
        with ExitStack() as part:
            c.x2 = scope(part)("x2", [128, NT, D], F32)
            c.h2_hi = scope(part)("h2_hi", [128, KT, NTOK], F32R)
            c.h2_lo = scope(part)("h2_lo", [128, KT, NTOK], F32R)
            with ExitStack() as inner, semaphores() as sem:
                out_projection(nc, scope(inner), sem, ins, c)
            with ExitStack() as inner, semaphores() as sem:
                mixer(nc, scope(inner), sem, ins, outs, c)
            with ExitStack() as inner, semaphores() as sem:
                final_norm(nc, scope(inner), sem, ins, outs, c)


MIXER_LINKS = 102
DVE_LINKS_HEADS = 59
ACT_LINKS_HEADS = 10


def kernel(**inputs):
    import concourse.bacc as bacc
    from concourse.bass_utils import run_bass_kernel_spmd

    nc = bacc.Bacc("TRN2", target_bir_lowering=False, num_devices=1)
    arrays, ins, outs = {}, {}, {}
    for name in INPUTS:
        arrays["in_" + name] = np.ascontiguousarray(inputs[name])
    arrays["in_bucket_onehot"] = bucket_onehot()
    arrays["in_pair_select"] = pair_select()
    for name, a in arrays.items():
        ins[name[3:]] = nc.dram_tensor(name, a.shape, mybir.dt.from_np(a.dtype), kind="ExternalInput").ap()
    for name, shape in OUTPUTS:
        outs[name] = nc.dram_tensor("out_" + name, shape, F32, kind="ExternalOutput").ap()
    build(nc, ins, outs)
    r = run_bass_kernel_spmd(nc, [arrays], core_ids=[0])
    return tuple(r.results[0]["out_" + name] for name, _ in OUTPUTS)
```
